# Optimizing a Trainium2 kernel written in Bass

```python
import jax, jax.numpy as jnp
from jax import lax
import numpy as np

D_MODEL = 1024
BATCH = 1
SEQ = 512
DEPTH = 1
DEC_BATCH = 8
DEC_SEQ = 1
PAST_LEN = 4096
PAGE_SIZE = 128

RET_HEADS = 4
RET_QK_DIM = D_MODEL // 16
RET_V_DIM = D_MODEL // 8
RET_WIDTH = RET_HEADS * RET_V_DIM
CHUNK = 128
ROPE_BASE = 10000.0
POOL_WINDOWS = (2, 4, 8, 16)
POOL_GROUPS = len(POOL_WINDOWS)
POOL_WIDTH = D_MODEL - RET_WIDTH
POOL_GROUP_DIM = POOL_WIDTH // POOL_GROUPS
POOL_BUF = max(POOL_WINDOWS) - 1
Q_W = RET_HEADS * RET_QK_DIM
K_W = RET_HEADS * RET_QK_DIM
V_W = RET_WIDTH
G_W = RET_WIDTH
IN_WIDTH = Q_W + K_W + V_W + G_W + POOL_WIDTH
SPLITS = [Q_W, Q_W + K_W, Q_W + K_W + V_W, Q_W + K_W + V_W + G_W]
MIX_WIDTH = RET_WIDTH + POOL_WIDTH
N_EXPERTS = 64
TOP_K = 8
N_EXPERT_GROUPS = 8
TOP_GROUPS = 4
EXPERT_DIM = D_MODEL // 4
SHARED_DIM = EXPERT_DIM
ROUTE_SCALE = 2.5
MOE_BLOCK = 1024
EPS = 1e-6

kernel_name = 'hybrid_retention_pool_moe_step'

def rmsnorm(x, g):
    xf = x.astype(jnp.float32)
    y = xf * lax.rsqrt(jnp.mean(xf * xf, axis=-1, keepdims=True) + EPS)
    return (y * g.astype(jnp.float32)).astype(x.dtype)

def rotary(x, pos):
    half = x.shape[-1] // 2
    freqs = ROPE_BASE ** (-jnp.arange(half, dtype=jnp.float32) / half)
    ang = pos[:, None] * freqs[None, :]
    cos = jnp.cos(ang)[None, :, None, :]
    sin = jnp.sin(ang)[None, :, None, :]
    x1, x2 = x[..., :half], x[..., half:]
    return jnp.concatenate([x1 * cos - x2 * sin, x1 * sin + x2 * cos], axis=-1)

def ret_log_decay():
    return jnp.log(1.0 - 2.0 ** (-5.0 - jnp.arange(RET_HEADS, dtype=jnp.float32)))

def retention_chunk(s0, q, k, v):
    c = q.shape[1]
    lg = ret_log_decay()
    idx = jnp.arange(c, dtype=jnp.float32)
    diff = idx[:, None] - idx[None, :]
    causal = diff >= 0
    dmat = jnp.where(causal[None], jnp.exp(lg[:, None, None] * jnp.where(causal, diff, 0.0)[None]), 0.0)
    scores = jnp.einsum('bihd,bjhd->bhij', q, k) * dmat[None]
    inner = jnp.einsum('bhij,bjhe->bihe', scores, v)
    cross_decay = jnp.exp(lg[None, :] * (idx[:, None] + 1.0))
    cross = jnp.einsum('bihd,bhde->bihe', q, s0) * cross_decay[None, :, :, None]
    tail_decay = jnp.exp(lg[None, :] * (c - 1.0 - idx)[:, None])
    s_new = jnp.exp(lg * c)[None, :, None, None] * s0 + jnp.einsum('bjhd,bjhe,jh->bhde', k, v, tail_decay)
    return inner + cross, s_new

def retention(q, k, v, s0, chunk):
    b, l, h, _ = q.shape
    nc = l // chunk

    def to_chunks(t):
        return jnp.moveaxis(t.reshape(b, nc, chunk, h, t.shape[-1]), 1, 0)

    def step(s, qkv):
        o, s_new = retention_chunk(s, *qkv)
        return s_new, o

    s_fin, o = lax.scan(step, s0, (to_chunks(q), to_chunks(k), to_chunks(v)))
    o = jnp.moveaxis(o, 0, 1).reshape(b, l, h, v.shape[-1])
    return o, s_fin

def pool_mix(u, buf, start, w_pool, pool_scale):
    b, l, _ = u.shape
    ext = jnp.concatenate([buf.astype(u.dtype), u], axis=1)
    extf = ext.astype(jnp.float32)
    cs = jnp.concatenate([jnp.zeros((b, 1, POOL_WIDTH), jnp.float32), jnp.cumsum(extf, axis=1)], axis=1)
    pos = start + jnp.arange(l, dtype=jnp.float32)
    hi = cs[:, POOL_BUF + 1:]
    groups = []
    for gi, w in enumerate(POOL_WINDOWS):
        sl = slice(gi * POOL_GROUP_DIM, (gi + 1) * POOL_GROUP_DIM)
        lo = cs[:, POOL_BUF + 1 - w:POOL_BUF + 1 - w + l, sl]
        cnt = jnp.minimum(pos + 1.0, float(w))
        groups.append((hi[..., sl] - lo) / cnt[None, :, None] - extf[:, POOL_BUF:, sl])
    p = jnp.stack(groups, axis=2)
    p = jnp.einsum('blgc,gcd->blgd', p, w_pool.astype(jnp.float32)).reshape(b, l, POOL_WIDTH)
    p = p * pool_scale.astype(jnp.float32)
    return p.astype(u.dtype), ext[:, -POOL_BUF:]

def mixer(h, s_ret, s_pool, start, chunk, w_in, w_out, w_pool, pool_scale):
    b, l, _ = h.shape
    proj = jnp.einsum('bld,de->ble', h, w_in)
    q, k, v, g, u = jnp.split(proj, SPLITS, axis=-1)
    pos = start + jnp.arange(l, dtype=jnp.float32)
    q = rotary(q.reshape(b, l, RET_HEADS, RET_QK_DIM).astype(jnp.float32), pos)
    k = rotary(k.reshape(b, l, RET_HEADS, RET_QK_DIM).astype(jnp.float32), pos) * (RET_QK_DIM ** -0.5)
    v = v.reshape(b, l, RET_HEADS, RET_V_DIM).astype(jnp.float32)
    o, s_new = retention(q, k, v, s_ret.astype(jnp.float32), chunk)
    mu = jnp.mean(o, axis=-1, keepdims=True)
    var = jnp.mean(jnp.square(o - mu), axis=-1, keepdims=True)
    o = ((o - mu) * lax.rsqrt(var + EPS)).reshape(b, l, RET_WIDTH)
    o = (jax.nn.silu(g.astype(jnp.float32)) * o).astype(h.dtype)
    p, buf_new = pool_mix(u, s_pool, start, w_pool, pool_scale)
    y = jnp.einsum('ble,ed->bld', jnp.concatenate([o, p], axis=-1), w_out)
    return y, s_new.astype(s_ret.dtype), buf_new.astype(s_pool.dtype)

def moe_block(t, w_router, router_bias, w_eg, w_eu, w_ed, w_sg, w_su, w_sd):
    n = t.shape[0]
    scores = jax.nn.sigmoid(jnp.dot(t.astype(jnp.float32), w_router.astype(jnp.float32)))
    biased = scores + router_bias.astype(jnp.float32)
    grp = biased.reshape(n, N_EXPERT_GROUPS, N_EXPERTS // N_EXPERT_GROUPS)
    grp_score = lax.top_k(grp, 2)[0].sum(-1)
    _, gidx = lax.top_k(grp_score, TOP_GROUPS)
    gmask = jax.nn.one_hot(gidx, N_EXPERT_GROUPS, dtype=jnp.float32).sum(1) > 0
    emask = jnp.repeat(gmask, N_EXPERTS // N_EXPERT_GROUPS, axis=-1)
    _, eidx = lax.top_k(jnp.where(emask, biased, -jnp.inf), TOP_K)
    sel = jnp.take_along_axis(scores, eidx, axis=-1)
    wts = sel / jnp.sum(sel, axis=-1, keepdims=True) * ROUTE_SCALE
    gates = jnp.einsum('tk,tke->te', wts, jax.nn.one_hot(eidx, N_EXPERTS, dtype=jnp.float32))
    hg = jnp.einsum('td,edf->tef', t, w_eg)
    hu = jnp.einsum('td,edf->tef', t, w_eu)
    a = jax.nn.silu(hg) * hu * gates.astype(t.dtype)[:, :, None]
    routed = jnp.einsum('tef,efd->td', a, w_ed)
    shared = jnp.dot(jax.nn.silu(jnp.dot(t, w_sg)) * jnp.dot(t, w_su), w_sd)
    return routed + shared

def moe(h, w_router, router_bias, w_eg, w_eu, w_ed, w_sg, w_su, w_sd):
    b, l, d = h.shape
    n = b * l
    blk = min(MOE_BLOCK, n)
    nb = -(-n // blk)
    flat = jnp.pad(h.reshape(n, d), ((0, nb * blk - n), (0, 0)))
    out = lax.map(lambda t: moe_block(t, w_router, router_bias, w_eg, w_eu, w_ed, w_sg, w_su, w_sd),
                  flat.reshape(nb, blk, d))
    return out.reshape(nb * blk, d)[:n].reshape(b, l, d)

def trunk(x, c, s_ret, s_pool, start, chunk, norm1, norm2, norm_f, w_ada, b_ada, w_in, w_out, w_pool,
          pool_scale, w_router, router_bias, w_eg, w_eu, w_ed, w_sg, w_su, w_sd):
    cs = jax.nn.silu(c)
    new_ret, new_pool = [], []
    for li in range(DEPTH):
        mod = jnp.dot(cs, w_ada[li]) + b_ada[li]
        sh1, sc1, g1, sh2, sc2, g2 = jnp.split(mod, 6, axis=-1)
        h = rmsnorm(x, norm1[li]) * (1.0 + sc1[:, None]) + sh1[:, None]
        y, r_new, p_new = mixer(h, s_ret[li], s_pool[li], start, chunk, w_in[li], w_out[li], w_pool[li], pool_scale[li])
        x = x + g1[:, None] * y
        h = rmsnorm(x, norm2[li]) * (1.0 + sc2[:, None]) + sh2[:, None]
        x = x + g2[:, None] * moe(h, w_router[li], router_bias[li], w_eg[li], w_eu[li], w_ed[li],
                                  w_sg[li], w_su[li], w_sd[li])
        new_ret.append(r_new)
        new_pool.append(p_new)
    return rmsnorm(x, norm_f), jnp.stack(new_ret), jnp.stack(new_pool)

def setup_inputs(seed: int = 0) -> dict:
    key = jax.random.key(seed)
    ks = jax.random.split(key, 28)
    f32 = jnp.float32

    def nrm(k, shape, scale):
        return jax.random.normal(k, shape, f32) * scale

    return {
        'x_prompt': nrm(ks[0], (BATCH, SEQ, D_MODEL), 1.0),
        'x_sample': nrm(ks[1], (DEC_BATCH, DEC_SEQ, D_MODEL), 1.0),
        'c_prompt': nrm(ks[2], (BATCH, D_MODEL), 1.0),
        'c_sample': nrm(ks[3], (DEC_BATCH, D_MODEL), 1.0),
        'state_ret': nrm(ks[4], (DEPTH, DEC_BATCH, RET_HEADS, RET_QK_DIM, RET_V_DIM), 1.0),
        'state_pool': nrm(ks[5], (DEPTH, DEC_BATCH, POOL_BUF, POOL_WIDTH), 1.0),
        'norm1': 1.0 + nrm(ks[6], (DEPTH, D_MODEL), 0.02),
        'norm2': 1.0 + nrm(ks[7], (DEPTH, D_MODEL), 0.02),
        'norm_f': 1.0 + nrm(ks[8], (D_MODEL,), 0.02),
        'w_ada': nrm(ks[9], (DEPTH, D_MODEL, 6 * D_MODEL), 0.02),
        'b_ada': nrm(ks[10], (DEPTH, 6 * D_MODEL), 0.02),
        'w_in': nrm(ks[11], (DEPTH, D_MODEL, IN_WIDTH), D_MODEL ** -0.5),
        'w_out': nrm(ks[12], (DEPTH, MIX_WIDTH, D_MODEL), MIX_WIDTH ** -0.5),
        'w_pool': nrm(ks[13], (DEPTH, POOL_GROUPS, POOL_GROUP_DIM, POOL_GROUP_DIM), POOL_GROUP_DIM ** -0.5),
        'pool_scale': 1.0 + nrm(ks[14], (DEPTH, POOL_WIDTH), 0.1),
        'w_router': nrm(ks[15], (DEPTH, D_MODEL, N_EXPERTS), D_MODEL ** -0.5),
        'router_bias': nrm(ks[16], (DEPTH, N_EXPERTS), 0.01),
        'w_exp_gate': nrm(ks[17], (DEPTH, N_EXPERTS, D_MODEL, EXPERT_DIM), D_MODEL ** -0.5),
        'w_exp_up': nrm(ks[18], (DEPTH, N_EXPERTS, D_MODEL, EXPERT_DIM), D_MODEL ** -0.5),
        'w_exp_down': nrm(ks[19], (DEPTH, N_EXPERTS, EXPERT_DIM, D_MODEL), EXPERT_DIM ** -0.5),
        'w_sh_gate': nrm(ks[20], (DEPTH, D_MODEL, SHARED_DIM), D_MODEL ** -0.5),
        'w_sh_up': nrm(ks[21], (DEPTH, D_MODEL, SHARED_DIM), D_MODEL ** -0.5),
        'w_sh_down': nrm(ks[22], (DEPTH, SHARED_DIM, D_MODEL), SHARED_DIM ** -0.5),
    }

def reference(x_prompt, x_sample, c_prompt, c_sample, state_ret, state_pool, norm1, norm2, norm_f,
              w_ada, b_ada, w_in, w_out, w_pool, pool_scale, w_router, router_bias, w_exp_gate,
              w_exp_up, w_exp_down, w_sh_gate, w_sh_up, w_sh_down):
    b = x_prompt.shape[0]
    zero_ret = jnp.zeros((DEPTH, b, RET_HEADS, RET_QK_DIM, RET_V_DIM), state_ret.dtype)
    zero_pool = jnp.zeros((DEPTH, b, POOL_BUF, POOL_WIDTH), state_pool.dtype)
    y_prompt, ret_p, pool_p = trunk(x_prompt, c_prompt, zero_ret, zero_pool, 0, min(CHUNK, x_prompt.shape[1]),
                                    norm1, norm2, norm_f, w_ada, b_ada, w_in, w_out, w_pool, pool_scale,
                                    w_router, router_bias, w_exp_gate, w_exp_up, w_exp_down,
                                    w_sh_gate, w_sh_up, w_sh_down)
    y_sample, ret_s, pool_s = trunk(x_sample, c_sample, state_ret, state_pool, PAST_LEN, x_sample.shape[1],
                                    norm1, norm2, norm_f, w_ada, b_ada, w_in, w_out, w_pool, pool_scale,
                                    w_router, router_bias, w_exp_gate, w_exp_up, w_exp_down,
                                    w_sh_gate, w_sh_up, w_sh_down)
    return (y_prompt, y_sample, ret_p, pool_p, ret_s, pool_s)


_drawn_inputs = setup_inputs


def setup_inputs(seed=0):
    import zlib

    import numpy as np

    out = dict(_drawn_inputs(seed))
    spreads = {}
    factors = {}
    for name, (base, spread) in spreads.items():
        noise = np.random.default_rng([zlib.crc32(name.encode()), seed]).standard_normal(out[name].shape)
        drawn = base * np.exp(spread * noise) if base else spread * noise
        out[name] = __import__('jax').numpy.asarray(drawn.astype(out[name].dtype))
    for name, factor in factors.items():
        out[name] = (out[name] * factor).astype(out[name].dtype)
    return out
```

```python
from contextlib import ExitStack

import numpy as np
import concourse.bass as bass
from concourse import mybir

F32 = mybir.dt.float32
I32 = mybir.dt.int32
ALU = mybir.AluOpType
ACT = mybir.ActivationFunctionType
AX_X = mybir.AxisListType.X
ds = bass.ds

P = 128
D = 1024
KD = D // P
SEQ = 512
NS = 8
NTOK = SEQ + NS
NT = 5
ROWS = [P, P, P, P, NS]
HALF = NTOK // 2
H = 4
QK = 64
VD = 128
POOL_W = (2, 4, 8, 16)
BUF = 15
PAD = 16
NE = 64
EF = 256
EPS = 1e-6
NCH = 12
ADA_ORDER = [0, 1, 2, 3, 8, 9, 4, 5, 6, 7, 10, 11]
TRASH = NTOK
ARENA = 53200
MAX_OVER = 32
NITEM = NE + MAX_OVER + 8
NO_SLOT = 640
NEG = -1.0e30

C_SIZES = dict(ident=P, rope=NT * 2 * 2 * QK, dmat=H * P, qdec=2 * P, kdec=H, gam=4, icnt=4 * 16,
               tri=P, ones=P, iota=NO_SLOT + P, tok=NT * 2, trash=2, before=64, rowok=NT,
               eye8=64, psel=P, ecol=1, bvals=8, islot=40, bm=4, bmul=4)
C_AT, _at = {}, 0
for _n, _s in C_SIZES.items():
    C_AT[_n] = _at
    _at += _s
C_W = _at


def constants():
    c = np.zeros((P, C_W), np.float32)

    def put(name, value):
        value = np.asarray(value, np.float64)
        value = value.reshape(value.shape[0], -1)
        c[:value.shape[0], C_AT[name]:C_AT[name] + value.shape[1]] = value

    p = np.arange(P)
    put("ident", np.eye(P))
    pos = np.zeros((P, NT))
    for t in range(4):
        pos[:, t] = t * P + p
    pos[:, 4] = 4096.0
    freq = (np.float32(10000.0) ** (-np.arange(32, dtype=np.float32) / np.float32(32))).astype(np.float32)
    ang = (pos[:, :, None].astype(np.float32) * freq[None, None]).astype(np.float32).astype(np.float64)
    rope = np.zeros((P, NT, 2, 2, QK))
    for i, scale in enumerate((1.0, QK ** -0.5)):
        rope[:, :, 0, i, :32] = rope[:, :, 0, i, 32:] = np.cos(ang) * scale
        rope[:, :, 1, i, :32] = -np.sin(ang) * scale
        rope[:, :, 1, i, 32:] = np.sin(ang) * scale
    put("rope", rope)
    lg = np.log(1.0 - 2.0 ** (-5.0 - np.arange(H)))
    d = p[None, :] - p[:, None]
    put("dmat", np.stack([np.where(d >= 0, np.exp(lg[h] * np.maximum(d, 0)), 0.0) for h in range(H)], 1))
    qd = np.zeros((P, 2, P))
    gam = np.zeros((P, 2, 2))
    for pair in range(2):
        for half in range(2):
            rows = slice(64 * half, 64 * half + 64)
            qd[rows, pair] = np.exp(lg[2 * pair + half] * (p + 1.0))
            gam[rows, 0, pair] = np.exp(lg[2 * pair + half] * P)
            gam[rows, 1, pair] = np.exp(lg[2 * pair + half])
    put("qdec", qd)
    put("gam", gam)
    put("kdec", np.exp(lg[None, :] * (P - 1.0 - p)[:, None]))
    icnt = np.zeros((P, 4, 16))
    for g, w in enumerate(POOL_W):
        icnt[:, g] = 1.0 / np.minimum(np.arange(16) + 1.0, w)
    put("icnt", icnt)
    put("tri", p[:, None] < p[None, :])
    put("ones", np.ones((P, P)))
    put("iota", np.tile(np.arange(NO_SLOT + P), (P, 1)))
    tok = np.zeros((P, NT, 2))
    tok[:, :, 0] = np.arange(NT)[None] * P + p[:, None]
    tok[:, :, 1] = 1.0
    put("tok", tok)
    put("trash", np.stack([-(TRASH + p), TRASH + p], 1))
    put("before", np.tile((np.arange(8)[None, :] < np.arange(8)[:, None]).reshape(1, 64), (P, 1)))
    put("rowok", (np.arange(NT)[None] * P + p[:, None]) < NTOK)
    put("eye8", np.tile(np.eye(8).reshape(1, 64), (P, 1)))
    put("psel", np.outer(p == NS, np.ones(P)))
    put("ecol", p[:, None])
    put("islot", np.tile(np.arange(40), (P, 1)))
    put("bm", np.tile(np.arange(4), (P, 1)))
    put("bmul", np.tile(128.0 * (np.arange(4) + 1), (P, 1)))
    return c


class Chain:

    def __init__(self, eng, sem, start=0):
        self.eng, self.sem, self.start, self.n = eng, sem, start, 0

    def do(self, ins):
        ins.then_inc(self.sem, 1)
        self.n += 1

    def settle(self):
        self.eng.wait_ge(self.sem, self.start + self.n)

    def link(self, ins):
        self.do(ins)
        self.settle()


def build(nc, I, O):
    ctx = ExitStack()
    with ctx:
        def sem(name):
            return ctx.enter_context(nc.semaphore(name))

        arena = ctx.enter_context(nc.sbuf_tensor("arena", [P, ARENA], F32))
        top = [0]
        names = [0]

        def view(at, shape, dt=F32, rows=P):
            n = int(np.prod(shape))
            v = arena[0:rows, at:at + n]
            if dt != F32:
                v = v.bitcast(dt)
            if len(shape) == 2:
                v = v.rearrange("p (a b) -> p a b", b=shape[1])
            elif len(shape) == 3:
                v = v.rearrange("p (a b c) -> p a b c", b=shape[1], c=shape[2])
            elif len(shape) == 4:
                v = v.rearrange("p (a b c d) -> p a b c d", b=shape[1], c=shape[2], d=shape[3])
            return v

        def place(n):
            at = top[0]
            top[0] += n
            assert top[0] <= ARENA, top[0]
            return at

        CST = place(C_W)
        x_sb = view(place(NT * D), (NT, D))
        mod_at = place(6 * D)
        mod = view(mod_at, (6 * D,))
        bcA_at, bcB_at, bcG_at = place(D), place(D), place(D)
        bcA, bcB, bcG = (view(a, (D,)) for a in (bcA_at, bcB_at, bcG_at))
        hT_at = place(KD * NTOK)
        hT = view(hT_at, (KD, NTOK))
        hb_at = place(2 * D)
        hb = view(hb_at, (2, D))
        M = place(4 * NTOK + 4 * (PAD + NTOK) + 4 * NTOK + 8 * NTOK)
        W = place(18432)
        SM = place(64)
        csT_at = place(9 * KD)

        def const(name, n=None, rows=P):
            n = C_SIZES[name] if n is None else n
            return arena[0:rows, CST + C_AT[name]:CST + C_AT[name] + n]

        ident = const("ident")
        rope = const("rope").rearrange("p (t c q d) -> p t c q d", t=NT, c=2, q=2)
        dmat = const("dmat").rearrange("p (h i) -> p h i", h=H)
        qdec = const("qdec").rearrange("p (a i) -> p a i", a=2)
        gam = const("gam").rearrange("p (s a) -> p s a", s=2)
        icnt = const("icnt").rearrange("p (g n) -> p g n", g=4)
        iota = const("iota")
        tokc = const("tok").rearrange("p (t c) -> p t c", t=NT)

        ada_at = [M, M + 4096, W, W + 4096, M] + 3 * [M + 8 * NTOK + 4 * (PAD + NTOK)] + 2 * [W, W + 4096]
        ada = [view(a, (KD, 512)) for a in ada_at]
        gT = view(M, (4, NTOK))
        uT = view(M + 4 * NTOK, (4, PAD + NTOK))
        pT = view(M + 4 * NTOK + 4 * (PAD + NTOK), (4, NTOK))
        catT = view(M + 8 * NTOK + 4 * (PAD + NTOK), (8, NTOK))
        xg = view(M, (2, D))
        xgT = [view(M + 2048 + i * 1024, (KD, P)) for i in range(2)]
        sel = [view(M + 4096 + i * 640, (NT, P)) for i in range(2)]
        act_sg = view(M + 5376, (2, EF))
        act_t = view(M + 5888, (2, EF))
        act_a = view(M + 6400, (2, EF))
        aT = view(M + 6912, (2, 2, P))
        Y = view(M + 7424, (2, D))
        w_qkv = view(W, (KD, 1024))
        w_gu = view(W + 8192, (KD, 1024))
        w_out = view(W, (KD, D))
        R0 = W + 8192
        v_sb = view(R0, (2, 512))
        qk_sb = view(R0 + 1024, (2, 512))
        rt = view(R0 + 2048, (2, 512))
        kd = view(R0 + 3072, (256,))
        qTz = view(R0 + 3328, (H, P))
        qTd = view(R0 + 3840, (H, P))
        kT = view(R0 + 4352, (2, P))
        scT = view(R0 + 4608, (H, P))
        St = view(R0 + 5120, (2, VD))
        on = view(R0 + 5376, (512,))
        w_pool = view(R0 + 5888, (4, P))
        pscale = view(R0 + 6400, (4,))
        S0 = view(W + 16384, (NS, 2, VD))
        nrm = view(W + 16384, (2, D), rows=9)
        pool_rows = [view(a, ((w - 1) * P,), rows=NS)
                     for a, w in zip((bcA_at + BUF * P, hb_at, bcG_at, bcA_at), POOL_W)]
        psum8 = view(hb_at + 1536, (512,), rows=NS)
        kd8 = view(hT_at, (NS, 256), rows=NS)
        qTm = view(hb_at, (H, 64))
        gu_w = [view(W + i * 4096, (KD, 512)) for i in range(2)]
        dn_w = [view(W + 8192 + i * 2048, (2, D)) for i in range(2)]
        sh_gu = view(W + 12288, (KD, 512))
        sh_dn = view(W + 16384, (2, D))
        squares = view(M, (D,))
        wo_g = view(M + D, (2, 512))
        squares_end = view(M + 5376, (D,))
        yin = view(hT_at, (2, D))
        yout = view(hb_at, (2, D))

        small = [SM]

        def tiny(shape, dt=F32, rows=P):
            at = small[0]
            small[0] += int(np.prod(shape))
            assert small[0] <= SM + 64
            return view(at, shape, dt, rows)

        csT = view(csT_at, (KD, 9))
        c_sb = view(hb_at, (D,), rows=9)
        c_sg = view(hb_at + D, (D,), rows=9)
        ss = tiny((8,))
        rstd = tiny((8,))
        bst = tiny((H, 6))
        mv = tiny((H, 2))
        lrs = tiny((H,))
        u8 = view(hb_at + 512, (512,), rows=NS)
        w_rt = view(W + 8192 + 3072, (KD, NE))
        small_route = W + 8192
        scores = view(small_route, (NT, NE))
        biased = view(small_route + 320, (NT, NE))
        rbias = view(small_route + 640, (NE,))
        top_a = view(small_route + 704, (40, 4))
        top_b = view(small_route + 864, (40, 4))
        top_c = view(small_route + 1024, (40, 2))
        top_d = view(small_route + 1104, (40, 2))
        top_e = view(small_route + 1184, (40, 2))
        top_f = view(small_route + 1264, (40, 2))
        gs = view(small_route + 1344, (NT, 8))
        rank = view(small_route + 1384, (NT, 8))
        cmp = view(small_route + 1424, (NT, 8, 8))
        cmp2 = view(small_route + 1744, (NT, 8, 8))
        v8 = view(small_route + 2064, (NT, 8))
        rep = view(small_route + 2104, (NT, NE))
        msk = view(small_route + 2424, (NT, NE))
        gsum = view(small_route + 2744, (8,))
        over = view(small_route + 2752, (4, 40), rows=NE)
        ov_w = view(small_route + 2912, (2, 40), rows=NE)
        cnt = view(small_route + 2992, (4,), rows=NE)
        present = view(small_route + 3000, (4,), rows=NE)
        place_o = view(small_route + 3008, (4,), rows=NE)
        rt_at = CST + C_AT["rope"]
        posm = view(rt_at, (NT, NE))
        gates = view(rt_at + 320, (NT, NE))
        table = view(rt_at + 640, (2, NITEM), I32, rows=1)
        tablef = view(bcA_at, (2, NITEM), rows=1)
        npair = view(rt_at + 640 + 2 * NITEM, (4,), I32, rows=1)
        info = [view(rt_at + 856 + 15 * i, (NT, 3)) for i in range(2)]
        gidx = view(rt_at + 890, (2,), I32)
        sidx = view(rt_at + 892, (2,), I32)
        got = view(rt_at + 894, (2, 3))
        tmpi = view(rt_at + 900, (1,))
        midx = view(rt_at + 901, (2,), I32)
        mgate = view(rt_at + 903, (2,))

        bank = [ctx.enter_context(nc.psum_tensor(f"bank{i}", [P, 512], F32)) for i in range(8)]

        h2_dram = nc.dram_tensor("h2_rows", (NTOK, D), F32).ap()
        sums = nc.dram_tensor("moe_sums", (NTOK + P, D), F32).ap()

        s_const, s_c, s_x, s_nrm = sem("const_in"), sem("c_in"), sem("x_in"), sem("norms_in")
        s_ada, s_bada = [sem(f"ada_in{i}") for i in range(4)], sem("ada_bias_in")
        s_wgu, s_wqkv, s_wout = sem("w_gu_in"), sem("w_qkv_in"), sem("w_out_in")
        s_wpool, s_state, s_rows = sem("w_pool_in"), sem("state_in"), sem("pool_rows_in")
        s_rt, s_shw, s_nf = sem("router_in"), sem("shared_in"), sem("norm_f_in")
        s_sig_c, s_cs, s_csT, s_csTs = sem("c_sigmoid"), sem("c_silu"), sem("cT_done"), sem("cT_in_sbuf")
        s_adam, s_modv = sem("ada_products"), sem("mod_rows")
        s_ssq, s_var, s_std, s_rstd = sem("x_squares"), sem("x_var"), sem("x_std"), sem("x_rstd")
        s_bcm, s_bcs = sem("broadcast_products"), sem("broadcast_in_sbuf")
        s_hb, s_hTm, s_hTs = sem("h_rows"), sem("hT_done"), sem("hT_in_sbuf")
        s_gum, s_gsig, s_gv, s_uv = sem("gu_products"), sem("g_sigmoid"), sem("g_silu"), sem("u_in_sbuf")
        s_qkvm, s_vs, s_rot, s_kd = sem("qkv_products"), sem("v_in_sbuf"), sem("qk_rotated"), sem("k_decayed")
        s_qkT, s_kTs, s_qTz, s_qTd = sem("qkT_done"), sem("kT_in_sbuf"), sem("qT_in_sbuf"), sem("qT_decayed")
        s_scm, s_sc, s_o, s_st, s_stv = sem("scores_done"), sem("scores_decayed"), sem("o_done"), sem("state_products"), sem("state_updated")
        s_lv, s_ls, s_on, s_oT, s_cat = sem("o_var"), sem("o_std"), sem("o_normed"), sem("oT_done"), sem("cat_o")
        s_pad, s_pool, s_pm, s_pc = sem("pads"), sem("pooled"), sem("pool_products"), sem("cat_p")
        s_u8m, s_u8, s_ulm, s_ul = sem("u8_done"), sem("u8_in_sbuf"), sem("u_last_done"), sem("u_last_in_sbuf")
        s_p8, s_p8m, s_p8s = sem("p8_rows"), sem("p8T_done"), sem("p8T_in_sbuf")
        s_k8, s_qm, s_outer, s_snew = sem("k_spread"), sem("q_spread"), sem("outer_products"), sem("sample_states")
        s_store, s_h2st, s_zero = sem("stores"), [sem(f"h2_rows_stored{i}") for i in range(2)], sem("zeros")
        s_wo, s_x2, s_ssq2, s_var2, s_std2 = sem("out_products"), sem("x2"), sem("x2_squares"), sem("x2_var"), sem("x2_std")
        s_rstd2 = sem("x2_rstd")
        s_h2, s_h2T, s_h2Ts = sem("h2_rows_made"), sem("h2T_done"), sem("h2T_in_sbuf")
        s_rm, s_scr, s_msk, s_posm, s_cntm = sem("router_products"), sem("scores"), sem("chosen"), sem("slot_sums"), sem("counts")
        s_cnt, s_ovx, s_ovm, s_ov, s_ovw, s_tm, s_table = (sem(n) for n in ("counts_in_sbuf", "extra_items", "extra_before", "extra_places", "extra_rows", "table_products", "table"))
        s_sel, s_selm, s_idx, s_sidx = sem("sel_ready"), sem("sel_done"), sem("idx_ready"), sem("scatter_idx")
        s_gat = [sem(f"gathered{i}") for i in range(2)]
        s_xT, s_xTs, s_gm, s_sg, s_a = sem("xT_done"), sem("xT_in_sbuf"), sem("gate_up_done"), sem("gate_sigmoid"), sem("a_ready")
        s_aT, s_aTs, s_dm, s_ya, s_yb = sem("aT_done"), sem("aT_in_sbuf"), sem("down_done"), sem("y_left"), sem("y_right")
        s_sca, s_ysh = sem("scattered"), [sem("shared_stored0"), sem("shared_stored1")]
        s_guw = [sem(f"gate_up_in{i}") for i in range(2)]
        s_dnw = [sem(f"down_in{i}") for i in range(2)]
        s_yin = [sem(f"sums_in{i}") for i in range(2)]
        s_x3, s_fs, s_fv, s_fsd, s_out = (sem(n) for n in ("x3", "x3_squares", "x3_var", "x3_std", "out_rows"))
        s_ost = [sem(f"out_stored{i}") for i in range(2)]
        s_dp, s_dl, s_de = sem("vector_steps"), sem("vector_loop_steps"), sem("vector_end_steps")
        s_ap, s_pp = sem("scalar_steps"), sem("pool_steps")
        s_init, s_zero_q, s_rzero = sem("sums_set"), sem("q_zeros"), sem("scores_set")

        def tcols(t):
            return slice(t * P, t * P + ROWS[t])

        def bv(i, *dims, rows=P):
            n = int(np.prod(dims))
            v = bank[i][0:rows, 0:n]
            if len(dims) == 2:
                v = v.rearrange("p (a b) -> p a b", b=dims[1])
            elif len(dims) == 3:
                v = v.rearrange("p (a b c) -> p a b c", b=dims[1], c=dims[2])
            return v

        def wait_y_free(eng, n, before):
            if before is not None:
                eng.wait_ge(s_sca, before * 16 + 16)
            elif n >= 2:
                eng.wait_ge(s_ysh[n % 2], 16 * ((n - 2) // 2 + 1))

        ADA_BANK = (1, 2, 1, 2, 3, 7, 3, 7, 3, 7, 4, 5)

        def seg(n, rows):
            return mod[0:rows, n * D:(n + 1) * D]

        blk = ctx.enter_context(nc.Block())

        @blk.sync
        def _(sp):
            sp.dma_start(c_sb[0:NS, :], I["c_sample"]).then_inc(s_c, 16)
            sp.dma_start(c_sb[NS:NS + 1, :], I["c_prompt"]).then_inc(s_c, 16)
            sp.dma_start(arena[:, CST:CST + C_W], I["consts"]).then_inc(s_const, 16)
            wa = I["w_ada"][0].rearrange("(p k) n -> p k n", k=KD)
            wi = I["w_in"][0].rearrange("(p k) n -> p k n", k=KD)

            def load_ada(c):
                at = ADA_ORDER[c] * 512
                sp.dma_start(ada[c], wa[:, :, at:at + 512]).then_inc(s_ada[c % 4], 16)

            load_ada(0)
            for t in range(4):
                sp.dma_start(x_sb[:, t, :], I["x_prompt"][0, t * P:(t + 1) * P, :]).then_inc(s_x, 16)
            sp.dma_start(x_sb[0:NS, 4, :], I["x_sample"].rearrange("b s d -> (b s) d")).then_inc(s_x, 16)
            sp.dma_start(mod[0:9, :], I["b_ada"][0].partition_broadcast(9)).then_inc(s_bada, 16)
            sp.dma_start(nrm[:, 0, :], I["norm1"][0].partition_broadcast(9)).then_inc(s_nrm, 16)
            sp.dma_start(nrm[:, 1, :], I["norm2"][0].partition_broadcast(9)).then_inc(s_nrm, 16)
            for c in range(1, 4):
                load_ada(c)
            sp.wait_ge(s_adam, 1)
            load_ada(4)
            sp.dma_start(w_gu, wi[:, :, 1024:2048]).then_inc(s_wgu, 16)
            sp.wait_ge(s_adam, 2)
            load_ada(5)
            sp.wait_ge(s_adam, 4)
            sp.dma_start(w_qkv, wi[:, :, 0:1024]).then_inc(s_wqkv, 16)
            sp.wait_ge(s_hb, NT)
            sp.wait_ge(s_hTm, NT)
            pool_in = I["state_pool"][0]
            for g, w in enumerate(POOL_W):
                sp.dma_start(pool_rows[g].rearrange("p (r c) -> p r c", c=P),
                             pool_in[:, BUF - w + 1:BUF, g * P:(g + 1) * P]).then_inc(s_rows, 16)
            sp.dma_start(O["pool_s"][0, :, 0:BUF - 1, :], pool_in[:, 1:BUF, :]).then_inc(s_store, 16)
            sp.wait_ge(s_adam, 6)
            load_ada(6)
            sp.wait_ge(s_modv, 6)
            for a in range(2):
                src = I["state_ret"][0].rearrange("s (a b) d v -> a b d s v", b=2)
                for b in range(2):
                    sp.dma_start(S0[64 * b:64 * b + 64, :, a, :], src[a, b]).then_inc(s_state, 16)
            sp.wait_ge(s_adam, 7)
            load_ada(7)
            sp.wait_ge(s_gum, 16)
            sp.dma_start(w_pool, I["w_pool"][0].rearrange("g c d -> c g d")).then_inc(s_wpool, 16)
            with nc.allow_non_contiguous_dma(reason="512 numbers, once"):
                sp.dma_start(pscale, I["pool_scale"][0].rearrange("(g p) -> p g", p=P)).then_inc(s_wpool, 16)
            sp.wait_ge(s_u8, 1)
            sp.dma_start(O["pool_s"][0, :, BUF - 1, :], u8).then_inc(s_store, 16)
            sp.wait_ge(s_ul, 1)
            sp.dma_start(O["pool_p"][0, 0], hb[0:BUF, 1, 0:512]).then_inc(s_store, 16)
            sp.wait_ge(s_qkvm, NT)
            load_ada(8)
            load_ada(9)
            sp.wait_ge(s_stv, 16)
            sp.dma_start(O["ret_p"][0, 0].rearrange("(a b) d v -> (b d) a v", b=2), St).then_inc(s_store, 16)
            wo = I["w_out"][0].rearrange("(k p) n -> p k n", p=P)
            for i in range(2):
                sp.wait_ge(s_adam, 9 + i)
                sp.dma_start(w_out[:, 4 * i:4 * i + 4, :], wo[:, 4 * i:4 * i + 4, :]).then_inc(s_wout, 16)
            sp.wait_ge(s_snew, 16)
            for a in range(2):
                dst = O["ret_s"][0].rearrange("s (a b) d v -> a b d s v", b=2)
                for b in range(2):
                    sp.dma_start(dst[a, b], S0[64 * b:64 * b + 64, :, a, :]).then_inc(s_store, 16)
            sp.wait_ge(s_cat, NT)
            sp.wait_ge(s_pm, 8)
            sp.wait_ge(s_pc, 8)
            sp.wait_ge(s_outer, 8)
            sp.wait_ge(s_o, NT)
            sp.wait_ge(s_store, 16 * 8)
            sp.dma_start(w_rt, I["w_router"][0].rearrange("(p k) e -> p k e", k=KD)).then_inc(s_rt, 16)
            sp.dma_start(rbias, I["router_bias"][0].partition_broadcast(P)).then_inc(s_rt, 16)
            for i, name in enumerate(("w_sh_gate", "w_sh_up")):
                sp.dma_start(sh_gu[:, :, i * EF:(i + 1) * EF],
                             I[name][0].rearrange("(p k) f -> p k f", k=KD)).then_inc(s_shw, 16)
            sp.dma_start(sh_dn, I["w_sh_down"][0].rearrange("(p k) n -> p k n", k=2)).then_inc(s_shw, 16)
            for t in range(NT):
                sp.wait_ge(s_h2, t + 1)
                sp.dma_start(h2_dram[t * P:t * P + ROWS[t], :], hb[0:ROWS[t], t % 2, :]).then_inc(s_h2st[t % 2], 16)
                if t == 2:
                    sp.wait_ge(s_wo, NT)
                    load_ada(10)
                    load_ada(11)

            eg = [I[n][0].rearrange("e (p k) f -> p e k f", k=KD) for n in ("w_exp_gate", "w_exp_up")]
            ed = I["w_exp_down"][0].rearrange("e (p k) n -> p e k n", k=2)

            def load_item(w, e, par):
                if not (isinstance(w, int) and w < 2):
                    sp.wait_ge(s_gm, w - 2 + NT + 1)
                for i in range(2):
                    sp.dma_start(gu_w[par][:, :, i * EF:(i + 1) * EF].unsqueeze(1), eg[i][:, ds(e, 1)]).then_inc(s_guw[par], 16)
                if not (isinstance(w, int) and w < 2):
                    sp.wait_ge(s_dm, w - 2 + NT + 1)
                sp.dma_start(dn_w[par].unsqueeze(1), ed[:, ds(e, 1)]).then_inc(s_dnw[par], 16)

            def store_shared(n):
                sp.wait_ge(s_ya, n + 1)
                sp.wait_ge(s_yb, n + 1)
                sp.dma_start(sums[n * P:n * P + ROWS[n], :], Y[0:ROWS[n], n % 2, :]).then_inc(s_ysh[n % 2], 16)

            sp.wait_ge(s_adam, NCH)
            for i in range(2):
                for w in range(2):
                    sp.dma_start(gu_w[w][:, :, i * EF:(i + 1) * EF].unsqueeze(1), eg[i][:, w:w + 1]).then_inc(s_guw[w], 16)
            sp.wait_ge(s_table, 1)
            for w in range(2):
                sp.dma_start(dn_w[w].unsqueeze(1), ed[:, w:w + 1]).then_inc(s_dnw[w], 16)
            for n in range(NT):
                store_shared(n)
            with sp.Fori(1, NE // 2 - 1) as i:
                for par in range(2):
                    load_item(i * 2 + par, i * 2 + par, par)
            sp.wait_ge(s_table, 1)
            more = sp.value_load(npair[0:1, 0:1], min_val=NE // 2 - 1, max_val=(NE + MAX_OVER - 1) // 2)
            with sp.Fori(NE // 2 - 1, more + 1) as i:
                for par in range(2):
                    e = sp.value_load(table[0:1, 0, ds(i * 2 + par, 1)], min_val=0, max_val=NE - 1)
                    load_item(i * 2 + par, e, par)
            sp.wait_ge(s_ya, more * 2 + (NT + 2))
            sp.wait_ge(s_yb, more * 2 + (NT + 2))
            sp.dma_start(bcA, I["norm_f"].partition_broadcast(P)).then_inc(s_nf, 16)
            sp.wait_ge(s_sca, more * 32 + 48)
            for t in range(NT):
                if t >= 2:
                    sp.wait_ge(s_x3, t - 1)
                sp.dma_start(yin[0:ROWS[t], t % 2, :], sums[t * P:t * P + ROWS[t], :]).then_inc(s_yin[t % 2], 16)
            for t in range(NT):
                sp.wait_ge(s_out, t + 1)
                dst = O["y_p"][0, t * P:(t + 1) * P, :] if t < 4 else O["y_s"].rearrange("b s d -> (b s) d")
                sp.dma_start(dst, yout[0:ROWS[t], t % 2, :]).then_inc(s_ost[t % 2], 16)
            sp.wait_ge(s_ost[0], 48)
            sp.wait_ge(s_ost[1], 32)
            sp.wait_ge(s_store, 16 * 8)

        @blk.gpsimd
        def _(pool):
            ch = Chain(pool, s_pp)
            pool.wait_ge(s_adam, 5)
            for g in range(4):
                ins = pool.memset(uT[:, g, 0:PAD], 0.0)
            ins.then_inc(s_pad, 1)
            L = PAD + SEQ
            wa = view(M + 8 * NTOK + 4 * (PAD + NTOK) + 4 * NTOK, (L,))
            wb = view(M + 8 * NTOK + 4 * (PAD + NTOK) + 5 * NTOK + 2 * PAD, (L,))
            pool.wait_ge(s_pad, 1)
            pool.wait_ge(s_uv, 8)
            pool.wait_ge(s_adam, 8)
            for g, w in enumerate(POOL_W):
                u = uT[:, g, :]
                src, step = u, 1
                for b in [wa, wb, wa, wb][:g + 1]:
                    ch.link(pool.tensor_tensor(b[:, 2 * step - 1:L], src[:, 2 * step - 1:L], src[:, step - 1:L - step], ALU.add))
                    src, step = b, step * 2
                ch.do(pool.tensor_scalar(pT[:, g, 16:SEQ], src[:, PAD + 16:L], 1.0 / w, None, ALU.mult))
                ch.link(pool.tensor_tensor(pT[:, g, 0:16], src[:, PAD:PAD + 16], icnt[:, g, :], ALU.mult))
                last = pool.tensor_tensor(pT[:, g, 0:SEQ], pT[:, g, 0:SEQ], u[:, PAD:L], ALU.subtract)
                last.then_inc(s_pool, 1)
                pool.wait_ge(s_pool, g + 1)
            pool.wait_ge(s_wo, NT)
            pool.wait_ge(s_x2, 2 * NT)
            pool.wait_ge(s_ssq2, NT)
            pool.memset(xg, 0.0).then_inc(s_zero, 1)
            pool.wait_ge(s_zero, 1)
            pool.dma_start(sums[TRASH:TRASH + P, :], xg[:, 0, :]).then_inc(s_sca, 16)
            pool.wait_ge(s_sca, 16)

            zero_reg, bound = pool.alloc_register("from_zero"), pool.alloc_register("row_bound")
            pool.reg_mov(zero_reg, 0)

            def gather(w, par):
                pool.wait_ge(s_idx, w + 1)
                if not (isinstance(w, int) and w < 2):
                    pool.wait_ge(s_xT, w - 1)
                pool.wait_ge(s_h2st[0], 48)
                pool.wait_ge(s_h2st[1], 32)
                pool.reg_add(bound, zero_reg, NTOK - 1)
                pool.indirect_dma_start(out=xg[:, par, :], out_offset=None, in_=h2_dram,
                                        in_offset=bass.IndirectOffsetOnAxis(ap=gidx[:, par:par + 1], axis=0),
                                        bounds_check=bound, oob_is_err=False).then_inc(s_gat[par], 16)

            def scatter(w, par):
                pool.wait_ge(s_sidx, w + 1)
                pool.wait_ge(s_ya, w + NT + 1)
                pool.wait_ge(s_yb, w + NT + 1)
                pool.wait_ge(s_sca, w * 16 + 16)
                pool.wait_ge(s_ysh[0], 16 * 3)
                pool.wait_ge(s_ysh[1], 16 * 2)
                pool.reg_add(bound, zero_reg, NTOK + P - 1)
                pool.indirect_dma_start(out=sums, out_offset=bass.IndirectOffsetOnAxis(ap=sidx[:, par:par + 1], axis=0),
                                        in_=Y[:, (par + NT) % 2, :], in_offset=None,
                                        bounds_check=bound, oob_is_err=True,
                                        compute_op=ALU.add).then_inc(s_sca, 16)

            gather(0, 0)
            gather(1, 1)
            gather(2, 0)
            gather(3, 1)
            scatter(0, 0)
            pool.wait_ge(s_table, 1)
            more = pool.value_load(npair[0:1, 0:1], min_val=NE // 2 - 1, max_val=(NE + MAX_OVER - 1) // 2)
            with pool.Fori(1, more + 1) as i:
                gather(i * 2 + 2, 0)
                scatter(i * 2 - 1, 1)
                gather(i * 2 + 3, 1)
                scatter(i * 2, 0)
            scatter(more * 2 + 1, 1)
            for par in range(2):
                pool.wait_ge(s_gat[par], more * 16 + 32)
            pool.wait_ge(s_sca, more * 32 + 48)

        @blk.tensor
        def _(pe):
            mm = pe.matmul
            pe.wait_ge(s_const, 16)
            pe.wait_ge(s_cs, 1)
            cv = c_sb.rearrange("p (q k) -> p k q", k=KD)
            for k in range(KD):
                ins = pe.transpose(bank[0][:, k * 9:(k + 1) * 9], cv[:, k, :], ident[0:9, 0:9])
            ins.then_inc(s_csT, 1)
            pe.wait_ge(s_csTs, 1)

            def ada_rows(c):
                pe.wait_ge(s_ada[c % 4], 16 * (c // 4 + 1))
                if c >= 2:
                    pe.wait_ge(s_modv, c - 1)
                for k in range(KD):
                    ins = mm(bank[ADA_BANK[c]][0:9, :], csT[:, k, :], ada[c][:, k, :], start=(k == 0), stop=(k == KD - 1))
                ins.then_inc(s_adam, 1)

            for c in range(4):
                ada_rows(c)

            def broadcast(n, i):
                for f in range(2):
                    if i > 0:
                        pe.wait_ge(s_bcs, 2 * (i - 1) + f + 1)
                    mm(bank[3 if f == 0 else 7][:, :], const("psel", rows=9), seg(n, 9)[:, f * 512:(f + 1) * 512],
                       start=True, stop=True).then_inc(s_bcm, 1)

            pe.wait_ge(s_modv, 4)
            broadcast(1, 0)
            broadcast(0, 1)

            def transposes(src, rows, banks, done):
                sv = src.rearrange("p (q k) -> p k q", k=KD)
                for k in range(KD):
                    b = bv(banks[k // 4], 4, rows)
                    ins = pe.transpose(b[:, k % 4, :], sv[:, k, :], ident[0:rows, 0:rows])
                ins.then_inc(done, 1)

            for t in range(NT):
                pe.wait_ge(s_hb, t + 1)
                if t >= 1:
                    pe.wait_ge(s_hTs, t)
                transposes(hb[0:ROWS[t], t % 2, :], ROWS[t], (4, 5), s_hTm)
                if t == 2:
                    ada_rows(4)
            pe.wait_ge(s_hTs, NT)
            pe.wait_ge(s_wgu, 16)
            GB = (0, 1, 2, 6)
            for i in range(16):
                n, f = i // 2, i % 2
                if 4 <= i < 12:
                    pe.wait_ge(s_gv, i - 3)
                elif i >= 12:
                    pe.wait_ge(s_uv, i - 11)
                for k in range(KD):
                    ins = mm(bank[GB[i % 4]][:, 0:HALF], w_gu[:, k, n * P:(n + 1) * P],
                             hT[:, k, f * HALF:(f + 1) * HALF], start=(k == 0), stop=(k == KD - 1))
                ins.then_inc(s_gum, 1)
                if i in (3, 7, 11):
                    ada_rows(5 + i // 4)

            def qkv(t, part):
                if part == 0:
                    if t == 0:
                        pe.wait_ge(s_wqkv, 16)
                        pe.wait_ge(s_uv, 8)
                        pe.wait_ge(s_bcs, 4)
                    if t >= 2:
                        pe.wait_ge(s_rot, t - 1)
                        pe.wait_ge(s_vs, t - 1)
                b = 2 * (t % 2)
                R = ROWS[t]
                for k in (2 * part, 2 * part + 1):
                    for f in range(2):
                        ins = mm(bank[b + f][0:R, :], hT[:, k, tcols(t)], w_qkv[:, k, f * 512:(f + 1) * 512],
                                 start=(k == 0), stop=(k == KD - 1))
                if part == 3:
                    ins.then_inc(s_qkvm, 1)

            def qk_transposes(t):
                R = ROWS[t]
                pe.wait_ge(s_rot, t + 1)
                if t >= 1:
                    pe.wait_ge(s_cat, t)
                else:
                    pe.wait_ge(s_u8, 1)
                b = bv(4, 4, R)
                for j in range(4):
                    ins = pe.transpose(b[:, j, :], qk_sb[0:R, t % 2, j * P:(j + 1) * P], ident[0:R, 0:R])
                ins.then_inc(s_qkT, 1)

            def retention_scores(t):
                pe.wait_ge(s_kTs, t + 1)
                pe.wait_ge(s_qTz, t + 1)
                pe.wait_ge(s_ul, 1)
                for h in range(H):
                    ins = mm(bank[5][:, h * P:(h + 1) * P], kT[:, h // 2, :], qTz[:, h, :], start=True, stop=True)
                ins.then_inc(s_scm, 1)

            def retention_out(t):
                pe.wait_ge(s_sc, t + 1)
                pe.wait_ge(s_vs, t + 1)
                pe.wait_ge(s_qTd, t + 1)
                if t >= 1:
                    pe.wait_ge(s_stv, 4 * t)
                    pe.wait_ge(s_on, t)
                for h in range(H):
                    o = bank[6][:, h * P:(h + 1) * P]
                    mm(o, scT[:, h, :], v_sb[:, t % 2, h * P:(h + 1) * P], start=True, stop=(t == 0))
                    if t >= 1:
                        ins = mm(o, qTd[:, h, :], St[:, h // 2, :], start=False, stop=True)
                pe.wait_ge(s_kd, t + 1)
                pe.wait_ge(s_p8s, 1)
                for a in range(2):
                    ins = mm(bank[7][:, a * 256:(a + 1) * 256], kd[:, a * P:(a + 1) * P],
                             v_sb[:, t % 2, a * 256:(a + 1) * 256], start=True, stop=True)
                ins.then_inc(s_o, 1)

            def o_transposes(t):
                R = ROWS[t]
                pe.wait_ge(s_on, t + 1)
                b = bv(4, 4, R)
                for h in range(H):
                    ins = pe.transpose(b[:, h, :], on[0:R, h * P:(h + 1) * P], ident[0:R, 0:R])
                ins.then_inc(s_oT, 1)

            qkv(0, 0)
            for g in range(4):
                ins = pe.transpose(bank[4][0:NS, g * P:(g + 1) * P], uT[:, g, PAD + SEQ:PAD + NTOK], ident)
            ins.then_inc(s_u8m, 1)
            for g in range(4):
                ins = pe.transpose(bank[5][0:BUF, g * P:(g + 1) * P], uT[:, g, PAD + SEQ - BUF:PAD + SEQ], ident)
            ins.then_inc(s_ulm, 1)
            for part in range(1, 4):
                qkv(0, part)
            pe.wait_ge(s_p8, 1)
            pe.wait_ge(s_modv, 8)
            b = bv(7, 4, NS)
            for g in range(4):
                ins = pe.transpose(b[:, g, :], psum8[:, g * P:(g + 1) * P], ident[0:NS, 0:NS])
            ins.then_inc(s_p8m, 1)
            for t in range(4):
                qkv(t + 1, 0)
                qk_transposes(t)
                qkv(t + 1, 1)
                retention_scores(t)
                qkv(t + 1, 2)
                retention_out(t)
                qkv(t + 1, 3)
                o_transposes(t)
            qk_transposes(4)
            pe.wait_ge(s_vs, 4)
            pe.wait_ge(s_stv, 16)
            broadcast(2, 2)
            broadcast(4, 3)

            def outer(i):
                a, s2 = i // 4, i % 4
                if i >= 2:
                    pe.wait_ge(s_snew, 2 * (i - 1))
                for j in range(2):
                    s = 2 * s2 + j
                    ins = mm(bank[i % 2][:, j * 256:(j + 1) * 256], kd8[:, s, a * P:(a + 1) * P],
                             v_sb[0:NS, 0, a * 256:(a + 1) * 256], start=True, stop=True)
                ins.then_inc(s_outer, 1)

            def pool_product(i):
                g, f = i // 2, i % 2
                if i >= 2:
                    pe.wait_ge(s_pc, i - 1)
                mm(bank[(2, 5)[i % 2]][:, 0:HALF], w_pool[:, g, :], pT[:, g, f * HALF:(f + 1) * HALF],
                   start=True, stop=True).then_inc(s_pm, 1)

            pe.wait_ge(s_k8, 1)
            pe.wait_ge(s_rot, 5)
            pe.wait_ge(s_vs, 5)
            outer(0)
            outer(1)
            pe.wait_ge(s_p8s, 1)
            pe.wait_ge(s_pool, 4)
            pe.wait_ge(s_wpool, 32)
            pe.wait_ge(s_sc, 4)
            for i in range(2, 8):
                pool_product(i - 2)
                outer(i)
            pool_product(6)
            pool_product(7)
            pe.wait_ge(s_bcs, 8)
            ada_rows(8)
            pe.wait_ge(s_snew, 16)
            pe.wait_ge(s_qm, 1)
            pe.wait_ge(s_on, 4)
            for h in range(H):
                for s in range(NS):
                    ins = mm(bank[6][0:NS, h * P:(h + 1) * P], qTm[:, h, s * 8:(s + 1) * 8], S0[:, s, h // 2, :],
                             start=(s == 0), stop=(s == NS - 1))
            ins.then_inc(s_o, 1)
            ada_rows(9)
            o_transposes(4)
            pe.wait_ge(s_modv, 10)
            broadcast(3, 4)

            def out_tile(t):
                b = 2 * ((t + 1) % 2)
                R = ROWS[t]
                if t >= 2:
                    pe.wait_ge(s_x2, 2 * (t - 1))
                for k in range(KD):
                    for f in range(2):
                        ins = mm(bank[b + f][0:R, :], catT[:, k, tcols(t)], w_out[:, k, f * 512:(f + 1) * 512],
                                 start=(k == 0), stop=(k == KD - 1))
                ins.then_inc(s_wo, 1)

            def h2_tile(t):
                R = ROWS[t]
                pe.wait_ge(s_h2, t + 1)
                if t >= 1:
                    pe.wait_ge(s_h2Ts, t)
                transposes(hb[0:R, t % 2, :], R, (4, 5), s_h2T)

            pe.wait_ge(s_pc, 8)
            pe.wait_ge(s_bcs, 10)
            pe.wait_ge(s_wout, 32)
            pe.wait_ge(s_cat, NT)
            out_tile(0)
            out_tile(1)
            h2_tile(0)
            out_tile(2)
            h2_tile(1)
            out_tile(3)
            h2_tile(2)
            out_tile(4)

            def gate_up(n, xT, wts, R, gb, part):
                for k in range(4 * part, 4 * part + 4):
                    ins = mm(bank[gb][0:R, :], xT[k], wts[:, k, :], start=(k == 0), stop=(k == KD - 1))
                if part == 1:
                    ins.then_inc(s_gm, 1)

            def a_transposes(n, R, par):
                pe.wait_ge(s_a, n + 1)
                if not (isinstance(n, int) and n == 0):
                    pe.wait_ge(s_aTs, n)
                av = act_a[0:R, par, :].rearrange("p (q k) -> p k q", k=2)
                for k in range(2):
                    ins = pe.transpose(bank[6][:, k * P:k * P + R], av[:, k, :], ident[0:R, 0:R])
                ins.then_inc(s_aT, 1)

            def down(n, R, par, wts):
                pe.wait_ge(s_aTs, n + 1)
                if not (isinstance(n, int) and n == 0):
                    pe.wait_ge(s_ya, n)
                    pe.wait_ge(s_yb, n)
                for f in range(2):
                    for k in range(2):
                        ins = mm(bank[2 + f][0:R, :], aT[:, par, k, 0:R], wts[:, k, f * 512:(f + 1) * 512],
                                 start=(k == 0), stop=(k == 1))
                ins.then_inc(s_dm, 1)

            def shared_gu(n, part):
                if part == 0:
                    pe.wait_ge(s_h2Ts, n + 1)
                    if n == 0:
                        pe.wait_ge(s_shw, 48)
                        pe.wait_ge(s_x2, 8)
                    if n >= 2:
                        pe.wait_ge(s_a, n - 1)
                gate_up(n, [hT[:, k, tcols(n)] for k in range(KD)], sh_gu, ROWS[n], n % 2, part)

            shared_gu(0, 0)
            h2_tile(3)
            shared_gu(0, 1)
            h2_tile(4)
            shared_gu(1, 0)
            pe.wait_ge(s_h2Ts, NT)
            pe.wait_ge(s_rt, 32)
            for t in range(NT):
                for k in range(KD):
                    ins = mm(bank[6][0:ROWS[t], t * NE:(t + 1) * NE], hT[:, k, tcols(t)], w_rt[:, k, :],
                             start=(k == 0), stop=(k == KD - 1))
            ins.then_inc(s_rm, 1)
            ada_rows(10)
            ada_rows(11)
            pe.wait_ge(s_msk, 1)
            for t in range(NT):
                for j in range(t + 1):
                    ins = mm(bank[7][:, t * NE:(t + 1) * NE], const("ones") if j < t else const("tri"), msk[:, j, :],
                             start=(j == 0), stop=(j == t))
            for t in range(NT):
                ins = mm(bank[7][0:NE, 320:321], msk[:, t, :], const("ones", 1), start=(t == 0), stop=(t == NT - 1))
            ins.then_inc(s_posm, 1)
            pe.wait_ge(s_scr, NT)
            shared_gu(1, 1)
            a_transposes(0, ROWS[0], 0)
            pe.wait_ge(s_ovx, 1)
            mm(bank[7][0:NE, 384:385], const("tri", NE, rows=NE), cnt[:, 1:2], start=True, stop=True).then_inc(s_ovm, 1)
            pe.wait_ge(s_x2, 10)
            down(0, ROWS[0], 0, sh_dn)
            shared_gu(2, 0)
            pe.wait_ge(s_ovw, 1)
            mm(bank[7][0:1, 388:428], const("ecol", rows=NE), ov_w[:, 0, :], start=True, stop=True)
            mm(bank[7][0:1, 428:468], const("ones", 1, rows=NE), ov_w[:, 1, :], start=True, stop=True)
            mm(bank[7][0:1, 468:469], cnt[:, 1:2], const("ones", 1, rows=NE), start=True, stop=True).then_inc(s_tm, 1)
            shared_gu(2, 1)
            a_transposes(1, ROWS[1], 1)
            down(1, ROWS[1], 1, sh_dn)

            def select(w, par):
                pe.wait_ge(s_sel, w + 1)
                if isinstance(w, int) and w == 0:
                    pe.wait_ge(s_table, 1)
                else:
                    pe.wait_ge(s_idx, w)
                for t in range(NT):
                    ins = mm(bank[7][:, 0:3], sel[par][:, t, :], info[par][:, t, :], start=(t == 0), stop=(t == NT - 1))
                ins.then_inc(s_selm, 1)

            def x_transposes(w, par):
                pe.wait_ge(s_gat[par], (w - par) * 8 + 16)
                if not (isinstance(w, int) and w == 0):
                    pe.wait_ge(s_xTs, w)
                transposes(xg[:, par, :], P, (4, 5), s_xT)

            def item(w, par, first=False):
                n = w + NT
                pe.wait_ge(s_xTs, w + 1)
                pe.wait_ge(s_guw[par], (w - par) * 16 + 32)
                pe.wait_ge(s_a, n - 1)
                xT = [xgT[par][:, k, :] for k in range(KD)]
                gate_up(n, xT, gu_w[par], P, (par + NT) % 2, 0)
                select(w + 2, par)
                R = ROWS[4] if first else P
                a_transposes(n - 1, R, (par + NT - 1) % 2)
                gate_up(n, xT, gu_w[par], P, (par + NT) % 2, 1)
                x_transposes(w + 1, 1 - par)
                if first:
                    down(n - 1, R, (par + NT - 1) % 2, sh_dn)
                else:
                    pe.wait_ge(s_dnw[1 - par], w * 8 + 8 * par)
                    down(n - 1, R, (par + NT - 1) % 2, dn_w[1 - par])

            shared_gu(3, 0)
            select(0, 0)
            shared_gu(3, 1)
            a_transposes(2, P, 0)
            down(2, P, 0, sh_dn)
            select(1, 1)
            shared_gu(4, 0)
            a_transposes(3, P, 1)
            shared_gu(4, 1)
            down(3, P, 1, sh_dn)
            pe.wait_ge(s_modv, NCH)
            x_transposes(0, 0)
            item(0, 0, first=True)
            item(1, 1)
            pe.wait_ge(s_table, 1)
            more = pe.value_load(npair[0:1, 0:1], min_val=NE // 2 - 1, max_val=(NE + MAX_OVER - 1) // 2)
            with pe.Fori(1, more + 1) as i:
                item(i * 2, 0)
                item(i * 2 + 1, 1)
            a_transposes(more * 2 + (NT + 1), P, 0)
            pe.wait_ge(s_dnw[1], more * 16 + 16)
            down(more * 2 + (NT + 1), P, 0, dn_w[1])
            pe.wait_ge(s_ya, more * 2 + (NT + 2))
            pe.wait_ge(s_yb, more * 2 + (NT + 2))
            pe.wait_ge(s_idx, more * 2 + 4)
            broadcast(5, 5)

        @blk.scalar
        def _(act):
            A = nc.scalar.activation
            ch = Chain(act, s_ap)
            act.wait_ge(s_c, 32)
            A(c_sg, c_sb, ACT.Sigmoid).then_inc(s_sig_c, 1)
            act.wait_ge(s_csT, 1)
            A(csT.rearrange("p k c -> p (k c)"), bank[0][:, 0:72], ACT.Copy).then_inc(s_csTs, 1)
            act.wait_ge(s_x, 16 * NT)
            act.wait_ge(s_init, 1)
            for t in range(NT):
                A(hT.rearrange("p k n -> p (k n)")[0:ROWS[t], 0:D], x_sb[0:ROWS[t], t, :], ACT.Square,
                  accum_out=ss[0:ROWS[t], t:t + 1]).then_inc(s_ssq, 1)
                act.wait_ge(s_ssq, t + 1)
            act.wait_ge(s_var, 1)
            A(rstd[:, 0:NT], rstd[:, 0:NT], ACT.Sqrt).then_inc(s_std, 1)

            def broadcast_copies(i, dst):
                for f in range(2):
                    act.wait_ge(s_bcm, 2 * i + f + 1)
                    A(dst[:, f * 512:(f + 1) * 512], bank[3 if f == 0 else 7][:, :], ACT.Copy).then_inc(s_bcs, 1)

            broadcast_copies(0, bcA)
            broadcast_copies(1, bcB)

            def hT_copies(R, t, done, dm):
                act.wait_ge(dm, t + 1)
                for i in range(2):
                    ins = A(hT[:, 4 * i:4 * i + 4, tcols(t)], bv(4 + i, 4, R), ACT.Copy)
                    ch.do(ins) if i == 0 else ins.then_inc(done, 1)

            for t in range(NT):
                hT_copies(ROWS[t], t, s_hTs, s_hTm)
            for i in range(16):
                n, f = i // 2, i % 2
                act.wait_ge(s_gum, i + 1)
                b = bank[(0, 1, 2, 6)[i % 4]][:, 0:HALF]
                if n < 4:
                    A(gT[:, n, f * HALF:(f + 1) * HALF], b, ACT.Sigmoid).then_inc(s_gsig, 1)
                else:
                    A(uT[:, n - 4, PAD + f * HALF:PAD + (f + 1) * HALF], b, ACT.Copy).then_inc(s_uv, 1)

            def v_copy(t):
                R = ROWS[t]
                act.wait_ge(s_qkvm, t + 1)
                if t >= 2:
                    act.wait_ge(s_o, t - 1)
                A(v_sb[0:R, t % 2, :], bank[2 * (t % 2) + 1][0:R, :], ACT.Copy).then_inc(s_vs, 1)

            def qkT_copies(t):
                R = ROWS[t]
                act.wait_ge(s_qkT, t + 1)
                if t >= 1:
                    act.wait_ge(s_scm, min(t, 4))
                    act.wait_ge(s_qTd, min(t, 4))
                b = bv(4, 4, R)
                qz = qTz.rearrange("p (a b) i -> p a b i", b=2)
                ch.do(A(qz[0:64, :, 0, 0:R], b[0:64, 0:2, :], ACT.Copy))
                A(qz[64:128, :, 1, 0:R], b[64:128, 0:2, :], ACT.Copy).then_inc(s_qTz, 1)
                A(kT[:, :, 0:R], b[:, 2:4, :], ACT.Copy).then_inc(s_kTs, 1)

            act.wait_ge(s_u8m, 1)
            A(u8, bank[4][0:NS, :], ACT.Copy).then_inc(s_u8, 1)
            act.wait_ge(s_ulm, 1)
            A(hb[0:BUF, 1, 0:512], bank[5][0:BUF, :], ACT.Copy).then_inc(s_ul, 1)
            act.wait_ge(s_zero_q, 1)
            v_copy(0)
            act.wait_ge(s_p8m, 1)
            A(pT[:, :, SEQ:NTOK], bv(7, 4, NS), ACT.Copy).then_inc(s_p8s, 1)
            for t in range(4):
                qkT_copies(t)
                act.wait_ge(s_lv, t + 1)
                A(lrs, lrs, ACT.Sqrt).then_inc(s_ls, 1)
                v_copy(t + 1)
            qkT_copies(4)
            act.wait_ge(s_p8, 1)
            broadcast_copies(2, bcG)
            broadcast_copies(3, bcA)
            act.wait_ge(s_wpool, 32)
            act.wait_ge(s_pool, 4)
            for i in range(8):
                g, f = i // 2, i % 2
                act.wait_ge(s_pm, i + 1)
                A(catT[:, 4 + g, f * HALF:(f + 1) * HALF], bank[(2, 5)[i % 2]][:, 0:HALF], ACT.Copy,
                  scale=pscale[:, g:g + 1]).then_inc(s_pc, 1)
            act.wait_ge(s_lv, 5)
            A(lrs[0:NS], lrs[0:NS], ACT.Sqrt).then_inc(s_ls, 1)
            broadcast_copies(4, bcB)
            for t in range(NT):
                R = ROWS[t]
                act.wait_ge(s_x2, 2 * t + 2)
                A(squares[0:R, :], x_sb[0:R, t, :], ACT.Square, accum_out=ss[0:R, t:t + 1]).then_inc(s_ssq2, 1)
                act.wait_ge(s_var2, t + 1)
                A(rstd[0:R, t:t + 1], rstd[0:R, t:t + 1], ACT.Sqrt).then_inc(s_std2, 1)
                if t >= 1:
                    hT_copies(ROWS[t - 1], t - 1, s_h2Ts, s_h2T)
            hT_copies(NS, 4, s_h2Ts, s_h2T)
            act.wait_ge(s_rm, 1)
            act.wait_ge(s_rzero, 1)
            for t in range(NT):
                R = ROWS[t]
                A(scores[0:R, t, :], bank[6][0:R, t * NE:(t + 1) * NE], ACT.Sigmoid).then_inc(s_scr, 1)

            def gate_sigmoid(n, R, par):
                act.wait_ge(s_gm, n + 1)
                if not (isinstance(n, int) and n < 2):
                    act.wait_ge(s_a, n - 1)
                A(act_sg[0:R, par, :], bank[par][0:R, 0:EF], ACT.Sigmoid).then_inc(s_sg, 1)

            def aT_copy(n, R, par):
                act.wait_ge(s_aT, n + 1)
                if not (isinstance(n, int) and n < 2):
                    act.wait_ge(s_dm, n - 1)
                A(aT[:, par, :, 0:R], bank[6][:, 0:256].rearrange("p (k r) -> p k r", k=2)[:, :, 0:R],
                  ACT.Copy).then_inc(s_aTs, 1)

            def y_copy(n, R, par, before=None):
                act.wait_ge(s_dm, n + 1)
                wait_y_free(act, n, before)
                A(Y[0:R, par, 0:512], bank[2][0:R, :], ACT.Copy).then_inc(s_ya, 1)

            def xT_copy(w, par):
                act.wait_ge(s_xT, w + 1)
                if not (isinstance(w, int) and w < 2):
                    act.wait_ge(s_gm, w + NT - 1)
                for i in range(2):
                    ins = A(xgT[par][:, 4 * i:4 * i + 4, :], bv(4 + i, 4, P), ACT.Copy)
                    if i == 1:
                        ins.then_inc(s_xTs, 1)

            gate_sigmoid(0, P, 0)
            aT_copy(0, P, 0)
            gate_sigmoid(1, P, 1)
            y_copy(0, P, 0)
            gate_sigmoid(2, P, 0)
            aT_copy(1, P, 1)
            y_copy(1, P, 1)
            gate_sigmoid(3, P, 1)
            aT_copy(2, P, 0)
            y_copy(2, P, 0)
            aT_copy(3, P, 1)
            gate_sigmoid(4, NS, 0)
            y_copy(3, P, 1)
            xT_copy(0, 0)

            def item(w, par, first=False):
                n = w + NT
                np_ = (par + NT) % 2
                R = NS if first else P
                aT_copy(n - 1, R, 1 - np_)
                gate_sigmoid(n, P, np_)
                xT_copy(w + 1, 1 - par)
                y_copy(n - 1, R, 1 - np_, None if isinstance(w, int) else w - 2)

            item(0, 0, first=True)
            item(1, 1)
            act.wait_ge(s_ysh[0], 16 * 3)
            act.wait_ge(s_table, 1)
            more = act.value_load(npair[0:1, 0:1], min_val=NE // 2 - 1, max_val=(NE + MAX_OVER - 1) // 2)
            with act.Fori(1, more + 1) as i:
                item(i * 2, 0)
                item(i * 2 + 1, 1)
            aT_copy(more * 2 + (NT + 1), P, 0)
            y_copy(more * 2 + (NT + 1), P, 0, more * 2)
            broadcast_copies(5, bcG)
            for t in range(NT):
                R = ROWS[t]
                act.wait_ge(s_x3, t + 1)
                A(squares_end[0:R, :], x_sb[0:R, t, :], ACT.Square, accum_out=ss[0:R, t:t + 1]).then_inc(s_fs, 1)
                act.wait_ge(s_fv, t + 1)
                A(rstd[0:R, t:t + 1], rstd[0:R, t:t + 1], ACT.Sqrt).then_inc(s_fsd, 1)

        @blk.vector
        def _(dve):
            V = nc.vector
            TT, TS, STT = V.tensor_tensor, V.tensor_scalar, V.scalar_tensor_tensor
            ch = Chain(dve, s_dp)
            V.memset(ss, 1.0).then_inc(s_init, 1)
            dve.wait_ge(s_sig_c, 1)
            TT(c_sb, c_sb, c_sg, ALU.mult).then_inc(s_cs, 1)
            dve.wait_ge(s_nrm, 32)
            dve.wait_ge(s_bada, 16)

            def add_ada(c):
                dve.wait_ge(s_adam, c + 1)
                n = ADA_ORDER[c]
                m = mod[0:9, n * 512:(n + 1) * 512]
                ins = TT(m, m, bank[ADA_BANK[c]][0:9, :], ALU.add)
                if n // 2 in (1, 4):
                    ch.link(ins)
                    norm = nrm[:, 0 if n // 2 == 1 else 1, (n % 2) * 512:(n % 2 + 1) * 512]
                    ins = STT(out=m, in0=m, scalar=1.0, in1=norm, op0=ALU.add, op1=ALU.mult)
                ins.then_inc(s_modv, 1)

            def variance(cols, squares_done, n, var_done, std_done, m):
                dve.wait_ge(squares_done, n)
                TS(rstd[:, cols], ss[:, cols], 1.0 / D, EPS, ALU.mult, ALU.add).then_inc(var_done, 1)
                dve.wait_ge(std_done, m)

            add_ada(0)
            variance(slice(0, NT), s_ssq, NT, s_var, s_std, 1)
            ch.link(V.reciprocal(rstd[:, 0:NT], rstd[:, 0:NT]))
            for c in range(1, 4):
                add_ada(c)

            def h_rows(t, scale, shift, done):
                R = ROWS[t]
                ch.link(STT(out=hb[0:R, t % 2, :], in0=x_sb[0:R, t, :], scalar=rstd[0:R, t:t + 1], in1=scale,
                            op0=ALU.mult, op1=ALU.mult))
                TT(hb[0:R, t % 2, :], hb[0:R, t % 2, :], shift, ALU.add).then_inc(done, 1)

            dve.wait_ge(s_bcs, 4)
            dve.wait_ge(s_modv, 4)
            for t in range(NT):
                if t >= 2:
                    dve.wait_ge(s_hTm, t - 1)
                h_rows(t, bcA if t < 4 else seg(1, NS), bcB if t < 4 else seg(0, NS), s_hb)
                if t == 3:
                    add_ada(4)
            for i in range(8):
                n, f = i // 2, i % 2
                dve.wait_ge(s_gsig, i + 1)
                g = gT[:, n, f * HALF:(f + 1) * HALF]
                TT(g, g, bank[(0, 1, 2, 6)[i % 4]][:, 0:HALF], ALU.mult).then_inc(s_gv, 1)
                if i in (3, 7):
                    add_ada(5 + i // 4)
            dve.wait_ge(s_rows, 64)
            for g in range(4):
                ch.do(V.tensor_reduce(psum8[:, g * P:(g + 1) * P], pool_rows[g].rearrange("p (r c) -> p c r", c=P), AX_X, ALU.add))
            add_ada(7)
            dve.wait_ge(s_gum, 16)
            ch.do(V.memset(qTz, 0.0))
            V.memset(St, 0.0).then_inc(s_zero_q, 1)
            dve.wait_ge(s_zero_q, 1)

            def rotate(t):
                R = ROWS[t]
                dve.wait_ge(s_qkvm, t + 1)
                src = bank[2 * (t % 2)][0:R, :].rearrange("p (c h d) -> p c h d", c=2, h=H)
                t1 = rt[0:R, 0, :].rearrange("p (c h d) -> p c h d", c=2, h=H)
                t2 = rt[0:R, 1, :].rearrange("p (c h d) -> p c h d", c=2, h=H)

                def turn(c, a, b):
                    return rope[0:R, t, c, :, a:b].unsqueeze(2).broadcast_to([R, 2, H, b - a])

                ch.do(TT(t1, src, turn(0, 0, QK), ALU.mult))
                ch.do(TT(t2[:, :, :, 0:32], src[:, :, :, 32:64], turn(1, 0, 32), ALU.mult))
                ch.link(TT(t2[:, :, :, 32:64], src[:, :, :, 0:32], turn(1, 32, 64), ALU.mult))
                TT(qk_sb[0:R, t % 2, :], rt[0:R, 0, :], rt[0:R, 1, :], ALU.add).then_inc(s_rot, 1)
                if t < 4:
                    dve.wait_ge(s_rot, t + 1)
                    TT(kd.rearrange("p (h d) -> p h d", h=H), qk_sb[:, t % 2, 256:512].rearrange("p (h d) -> p h d", h=H),
                       const("kdec").unsqueeze(2).broadcast_to([P, H, QK]), ALU.mult).then_inc(s_kd, 1)

            def o_norm_start(t):
                R = ROWS[t]
                for h in range(H):
                    ch.do(V.bn_stats(bst[0:R, h, :], bank[6][0:R, h * P:(h + 1) * P]))
                ch.settle()
                for h in range(H):
                    ch.do(V.bn_aggr(mv[0:R, h, :], bst[0:R, h, :]))
                ch.settle()
                TS(lrs[0:R, :], mv[0:R, :, 1], EPS, None, ALU.add).then_inc(s_lv, 1)

            def o_norm_end(t):
                R = ROWS[t]
                dve.wait_ge(s_ls, t + 1)
                ch.link(V.reciprocal(lrs[0:R, :], lrs[0:R, :]))
                if t >= 1:
                    dve.wait_ge(s_oT, t)
                for h in range(H):
                    ins = TS(on[0:R, h * P:(h + 1) * P], bank[6][0:R, h * P:(h + 1) * P], mv[0:R, h, 0:1], lrs[0:R, h:h + 1],
                             ALU.subtract, ALU.mult)
                    ch.do(ins) if h < 3 else ins.then_inc(s_on, 1)

            def gate_o(t):
                R = ROWS[t]
                dve.wait_ge(s_oT, t + 1)
                TT(catT[:, 0:4, tcols(t)], bv(4, 4, R), gT[:, :, tcols(t)], ALU.mult).then_inc(s_cat, 1)

            dve.wait_ge(s_u8, 1)
            ch.settle()
            ch.link(TT(psum8, psum8, u8, ALU.add))
            for g, w in enumerate(POOL_W):
                c = slice(g * P, (g + 1) * P)
                ins = STT(out=psum8[:, c], in0=psum8[:, c], scalar=1.0 / w, in1=u8[:, c], op0=ALU.mult, op1=ALU.subtract)
                ch.do(ins) if g < 3 else ins.then_inc(s_p8, 1)
            dve.wait_ge(s_gv, 8)
            rotate(0)
            for t in range(4):
                dve.wait_ge(s_qTz, t + 1)
                if t >= 1:
                    dve.wait_ge(s_o, t)
                TT(qTd.rearrange("p (a b) i -> p a b i", b=2), qTz.rearrange("p (a b) i -> p a b i", b=2),
                   qdec.unsqueeze(2).broadcast_to([P, 2, 2, P]), ALU.mult).then_inc(s_qTd, 1)
                dve.wait_ge(s_scm, t + 1)
                TT(scT, bv(5, 4, P), dmat, ALU.mult).then_inc(s_sc, 1)
                dve.wait_ge(s_o, t + 1)
                o_norm_start(t)
                if t >= 1:
                    dve.wait_ge(s_stv, 4 * t)
                for a in range(2):
                    for b in range(2):
                        r = slice(64 * b, 64 * b + 64)
                        STT(out=St[r, a, :], in0=St[r, a, :], scalar=gam[r, 0, a:a + 1],
                            in1=bank[7][r, a * 256 + b * P:a * 256 + (b + 1) * P], op0=ALU.mult, op1=ALU.add).then_inc(s_stv, 1)
                o_norm_end(t)
                rotate(t + 1)
                if t == 3:
                    dve.wait_ge(s_rot, 5)
                    TT(kd8, qk_sb[0:NS, 0, 256:512].unsqueeze(1).broadcast_to([NS, NS, 256]),
                       ident[0:NS, 0:NS].unsqueeze(2).broadcast_to([NS, NS, 256]), ALU.mult).then_inc(s_k8, 1)
                gate_o(t)
            dve.wait_ge(s_qTz, 5)
            TT(qTm.rearrange("p h (s m) -> p h s m", m=8), qTz[:, :, 0:NS].unsqueeze(2).broadcast_to([P, H, 8, 8]),
               const("eye8").rearrange("p (s m) -> p s m", m=8).unsqueeze(1).broadcast_to([P, H, 8, 8]), ALU.mult).then_inc(s_qm, 1)
            dve.wait_ge(s_state, 64)
            for i in range(8):
                a, s2 = i // 4, i % 4
                dve.wait_ge(s_outer, i + 1)
                bo = bv(i % 2, 2, 256)
                for b in range(2):
                    r = slice(64 * b, 64 * b + 64)
                    s_new = S0[r, 2 * s2:2 * s2 + 2, a, :]
                    STT(out=s_new, in0=s_new, scalar=gam[r, 1, a:a + 1], in1=bo[r, :, b * P:(b + 1) * P],
                        op0=ALU.mult, op1=ALU.add).then_inc(s_snew, 1)
            add_ada(8)
            dve.wait_ge(s_o, 5)
            o_norm_start(4)
            o_norm_end(4)
            add_ada(9)
            gate_o(4)
            V.memset(scores, 0.0).then_inc(s_rzero, 1)

            dve.wait_ge(s_bcs, 10)
            dve.wait_ge(s_modv, 10)
            dve.wait_ge(s_cat, NT)
            dve.wait_ge(s_store, 16 * 8)
            for t in range(NT):
                R = ROWS[t]
                dve.wait_ge(s_wo, t + 1)
                g1 = bcG if t < 4 else seg(2, NS)
                for f in range(2):
                    c = slice(f * 512, (f + 1) * 512)
                    ch.do(TT(wo_g[0:R, f, :], bank[2 * ((t + 1) % 2) + f][0:R, :], g1[:, c], ALU.mult))
                ch.settle()
                for f in range(2):
                    c = slice(f * 512, (f + 1) * 512)
                    TT(x_sb[0:R, t, c], x_sb[0:R, t, c], wo_g[0:R, f, :], ALU.add).then_inc(s_x2, 1)
                variance(slice(t, t + 1), s_ssq2, t + 1, s_var2, s_std2, t + 1)
                ch.link(V.reciprocal(rstd[:, t:t + 1], rstd[:, t:t + 1]))
                if t >= 2:
                    dve.wait_ge(s_h2T, t - 1)
                    dve.wait_ge(s_h2st[t % 2], 16 * (t // 2))
                h_rows(t, bcA if t < 4 else seg(4, NS), bcB if t < 4 else seg(3, NS), s_h2)

            dve.wait_ge(s_scr, NT)
            dve.wait_ge(s_rt, 32)
            ch.link(TT(biased, scores, rbias.unsqueeze(1).broadcast_to([P, NT, NE]), ALU.add))
            g8 = biased.rearrange("p t (g m) -> p (t g) m", m=8)
            ch.do(TT(top_a, g8[:, :, 0:4], g8[:, :, 4:8], ALU.max))
            ch.link(TT(top_b, g8[:, :, 0:4], g8[:, :, 4:8], ALU.min))
            ch.do(TT(top_c, top_a[:, :, 0:2], top_a[:, :, 2:4], ALU.max))
            ch.do(TT(top_d, top_a[:, :, 0:2], top_a[:, :, 2:4], ALU.min))
            ch.link(TT(top_e, top_b[:, :, 0:2], top_b[:, :, 2:4], ALU.max))
            ch.link(TT(top_d, top_d, top_e, ALU.max))
            ch.do(TT(top_f[:, :, 0:1], top_c[:, :, 0:1], top_c[:, :, 1:2], ALU.min))
            ch.do(TT(top_f[:, :, 1:2], top_d[:, :, 0:1], top_d[:, :, 1:2], ALU.max))
            ch.do(TT(top_e[:, :, 0:1], top_c[:, :, 0:1], top_c[:, :, 1:2], ALU.max))
            ch.settle()
            ch.link(TT(top_e[:, :, 1:2], top_f[:, :, 0:1], top_f[:, :, 1:2], ALU.max))
            gflat = gs.rearrange("p t g -> p (t g)").unsqueeze(2)
            ch.link(TT(gflat, top_e[:, :, 0:1], top_e[:, :, 1:2], ALU.add))
            mine = gs.unsqueeze(3).broadcast_to([P, NT, 8, 8])
            other = gs.unsqueeze(2).broadcast_to([P, NT, 8, 8])
            ch.do(TT(cmp, other, mine, ALU.is_gt))
            ch.link(TT(cmp2, other, mine, ALU.is_equal))
            ch.link(TT(cmp2, cmp2, const("before").rearrange("p (a b) -> p a b", b=8).unsqueeze(1).broadcast_to([P, NT, 8, 8]), ALU.mult))
            ch.link(TT(cmp, cmp, cmp2, ALU.add))
            ch.link(V.tensor_reduce(rank, cmp, AX_X, ALU.add))
            ch.link(TS(rank, rank, 3.5, NEG, ALU.is_gt, ALU.mult))
            ch.link(TT(g8, g8, rank.rearrange("p t g -> p (t g)").unsqueeze(2).broadcast_to([P, 40, 8]), ALU.add))
            for t in range(NT):
                ch.do(V.max(v8[:, t, :], biased[:, t, :]))
            ch.settle()
            for t in range(NT):
                ch.do(V.match_replace(rep[:, t, :], v8[:, t, :], biased[:, t, :], 3.0 * NEG))
            ch.settle()
            ch.link(TT(rep, rep, biased, ALU.not_equal))
            TT(msk, rep, const("rowok").unsqueeze(2).broadcast_to([P, NT, NE]), ALU.mult).then_inc(s_msk, 1)

            def gated(n, R, par, gate=None):
                dve.wait_ge(s_sg, n + 1)
                if not (isinstance(n, int) and n < 2):
                    dve.wait_ge(s_aT, n - 1)
                c = loop[0]
                c.link(TT(act_t[0:R, par, :], act_sg[0:R, par, :], bank[par][0:R, 0:EF], ALU.mult))
                if gate is None:
                    ins = TT(act_a[0:R, par, :], act_t[0:R, par, :], bank[par][0:R, EF:2 * EF], ALU.mult)
                else:
                    ins = STT(out=act_a[0:R, par, :], in0=act_t[0:R, par, :], scalar=gate, in1=bank[par][0:R, EF:2 * EF],
                              op0=ALU.mult, op1=ALU.mult)
                ins.then_inc(s_a, 1)

            def y_copy(n, R, par, before=None):
                dve.wait_ge(s_dm, n + 1)
                wait_y_free(dve, n, before)
                V.tensor_copy(Y[0:R, par, 512:1024], bank[3][0:R, :]).then_inc(s_yb, 1)

            loop = [ch]
            gated(0, P, 0)
            add_ada(10)
            add_ada(11)
            dve.wait_ge(s_msk, 1)
            ch.link(TT(gates, scores, msk, ALU.mult))
            ch.link(V.tensor_reduce(gsum[:, 0:NT], gates, AX_X, ALU.add))
            ch.link(TS(gsum[:, 0:NT], gsum[:, 0:NT], 1e-30, None, ALU.max))
            ch.link(V.reciprocal(gsum[:, 0:NT], gsum[:, 0:NT]))
            ch.link(TT(gates, gates, gsum[:, 0:NT].unsqueeze(2).broadcast_to([P, NT, NE]), ALU.mult))
            ch.link(TS(gates, gates, 2.5, None, ALU.mult))
            dve.wait_ge(s_posm, 1)
            pos_bank = bank[7][:, 0:NT * NE].rearrange("p (t e) -> p t e", e=NE)
            ch.link(STT(out=posm.rearrange("p t e -> p (t e)"), in0=bank[7][:, 0:NT * NE], scalar=1.0,
                        in1=msk.rearrange("p t e -> p (t e)"), op0=ALU.add, op1=ALU.mult))
            ch.link(TS(posm, posm, 1.0, None, ALU.subtract))
            ch.link(V.tensor_copy(cnt[:, 0:1], bank[7][0:NE, 320:321]))
            ch.link(TT(present, cnt[:, 0:1].broadcast_to([NE, 4]), const("bmul", rows=NE), ALU.is_gt))
            V.tensor_reduce(cnt[:, 1:2], present, AX_X, ALU.add).then_inc(s_ovx, 1)
            gated(1, P, 1)
            y_copy(0, P, 0)
            dve.wait_ge(s_ovm, 1)
            ch.link(V.tensor_copy(cnt[:, 2:3], bank[7][0:NE, 384:385]))
            ch.link(TS(place_o, const("bm", rows=NE), cnt[:, 2:3], None, ALU.add))
            ch.link(TT(over, const("islot", rows=NE).unsqueeze(1).broadcast_to([NE, 4, 40]),
                       place_o.unsqueeze(2).broadcast_to([NE, 4, 40]), ALU.is_equal))
            ch.link(TT(over, over, present.unsqueeze(2).broadcast_to([NE, 4, 40]), ALU.mult))
            ch.link(V.tensor_reduce(ov_w[:, 0, :], over.rearrange("p b s -> p s b"), AX_X, ALU.add))
            ch.link(TS(place_o, const("bmul", rows=NE), float(NO_SLOT), None, ALU.subtract))
            ch.link(TT(over, over, place_o.unsqueeze(2).broadcast_to([NE, 4, 40]), ALU.mult))
            V.tensor_reduce(ov_w[:, 1, :], over.rearrange("p b s -> p s b"), AX_X, ALU.add).then_inc(s_ovw, 1)
            ch.do(V.tensor_copy(tablef[:, 0, 0:NE], const("iota", NE, rows=1)))
            ch.do(V.memset(tablef[:, 1, 0:NE], 0.0))
            dve.wait_ge(s_tm, 1)
            ch.do(V.tensor_copy(tablef[:, 0, NE:NITEM], bank[7][0:1, 388:428]))
            ch.do(TS(tablef[:, 1, NE:NITEM], bank[7][0:1, 428:468], float(NO_SLOT), None, ALU.add))
            ch.do(TS(npair[:, 1:2], bank[7][0:1, 468:469], 1.0, None, ALU.add))
            ch.settle()
            ch.do(V.tensor_copy(table, tablef))
            ch.do(TS(npair[:, 2:3], npair[:, 1:2], 1, None, ALU.logical_shift_right))
            for i in range(2):
                ch.do(V.tensor_copy(info[i][:, :, 0:2], tokc))
            ch.settle()
            TS(npair[:, 0:1], npair[:, 2:3], float(NE // 2 - 1), None, ALU.add).then_inc(s_table, 1)
            dve.wait_ge(s_table, 1)

            def choose(w, par, e, base):
                if not (isinstance(w, int) and w < 2):
                    dve.wait_ge(s_selm, w - 1)
                c = loop[0]
                c.do(TT(sel[par], iota[:, ds(base, P)].unsqueeze(1).broadcast_to([P, NT, P]),
                        posm[:, :, ds(e, 1)].broadcast_to([P, NT, P]), ALU.is_equal))
                V.tensor_copy(info[par][:, :, 2:3], gates[:, :, ds(e, 1)]).then_inc(s_sel, 1)

            def rows_of(w, par):
                dve.wait_ge(s_selm, w + 1)
                if not (isinstance(w, int) and w < 2):
                    dve.wait_ge(s_gat[par], (w - par) * 8)
                c = loop[0]
                c.link(V.tensor_copy(got[:, par, :], bank[7][:, 0:3]))
                c.link(TS(tmpi, got[:, par, 1:2], const("trash")[:, 0:1], const("trash")[:, 1:2], ALU.mult, ALU.add))
                TT(gidx[:, par:par + 1], tmpi, got[:, par, 0:1], ALU.add).then_inc(s_idx, 1)

            def take_rows(w, par):
                dve.wait_ge(s_idx, w + 1)
                if not (isinstance(w, int) and w < 2):
                    dve.wait_ge(s_sidx, w - 1)
                    dve.wait_ge(s_a, w + NT - 1)
                c = loop[0]
                c.do(V.tensor_copy(midx[:, par:par + 1], gidx[:, par:par + 1]))
                c.link(V.tensor_copy(mgate[:, par:par + 1], got[:, par, 2:3]))

            def keep_rows(w, par):
                if not (isinstance(w, int) and w < 2):
                    dve.wait_ge(s_sca, (w - 1) * 16 + 16)
                V.tensor_copy(sidx[:, par:par + 1], midx[:, par:par + 1]).then_inc(s_sidx, 1)

            choose(0, 0, 0, 0)
            choose(1, 1, 1, 0)
            gated(2, P, 0)
            y_copy(1, P, 1)
            rows_of(0, 0)
            choose(2, 0, 2, 0)
            gated(3, P, 1)
            y_copy(2, P, 0)
            rows_of(1, 1)
            gated(4, NS, 0)
            y_copy(3, P, 1)

            def item(w, par, first=False):
                n = w + NT
                np_ = (par + NT) % 2
                take_rows(w, par)
                rows_of(w + 2, par)
                gated(n, P, np_, mgate[:, par:par + 1])
                y_copy(n - 1, NS if first else P, 1 - np_, None if isinstance(w, int) else w - 2)
                keep_rows(w, par)
                if isinstance(w, int):
                    choose(w + 3, 1 - par, w + 3, 0)
                else:
                    e = dve.value_load(table[0:1, 0, ds(w + 3, 1)], min_val=0, max_val=NE - 1)
                    base = dve.value_load(table[0:1, 1, ds(w + 3, 1)], min_val=0, max_val=NO_SLOT)
                    choose(w + 3, 1 - par, e, base)

            item(0, 0, first=True)
            item(1, 1)
            more = dve.value_load(npair[0:1, 0:1], min_val=NE // 2 - 1, max_val=(NE + MAX_OVER - 1) // 2)
            dve.wait_ge(s_ysh[0], 16 * 3)
            STEPS = 12
            with dve.Fori(1, more + 1) as i:
                loop[0] = Chain(dve, s_dl, i * STEPS - STEPS)
                item(i * 2, 0)
                item(i * 2 + 1, 1)
                assert loop[0].n == STEPS, loop[0].n
            y_copy(more * 2 + (NT + 1), P, 0, more * 2)

            ch = Chain(dve, s_de)
            dve.wait_ge(s_bcs, 12)
            dve.wait_ge(s_nf, 16)
            dve.wait_ge(s_h2st[0], 48)
            dve.wait_ge(s_h2st[1], 32)
            for t in range(NT):
                R = ROWS[t]
                dve.wait_ge(s_yin[t % 2], 16 * (t // 2 + 1))
                y = yin[0:R, t % 2, :]
                ch.link(TT(y, y, bcG if t < 4 else seg(5, NS), ALU.mult))
                TT(x_sb[0:R, t, :], x_sb[0:R, t, :], y, ALU.add).then_inc(s_x3, 1)
                variance(slice(t, t + 1), s_fs, t + 1, s_fv, s_fsd, t + 1)
                ch.link(V.reciprocal(rstd[:, t:t + 1], rstd[:, t:t + 1]))
                if t >= 2:
                    dve.wait_ge(s_ost[t % 2], 16 * (t // 2))
                STT(out=yout[0:R, t % 2, :], in0=x_sb[0:R, t, :], scalar=rstd[0:R, t:t + 1], in1=bcA[0:R, :],
                    op0=ALU.mult, op1=ALU.mult).then_inc(s_out, 1)


_INS = ["x_prompt", "x_sample", "c_prompt", "c_sample", "state_ret", "state_pool", "norm1", "norm2", "norm_f",
        "w_ada", "b_ada", "w_in", "w_out", "w_pool", "pool_scale", "w_router", "router_bias",
        "w_exp_gate", "w_exp_up", "w_exp_down", "w_sh_gate", "w_sh_up", "w_sh_down"]
_OUTS = {"y_p": (1, SEQ, D), "y_s": (NS, 1, D), "ret_p": (1, 1, H, QK, VD), "pool_p": (1, 1, BUF, 512),
         "ret_s": (1, NS, H, QK, VD), "pool_s": (1, NS, BUF, 512)}


def kernel(**inputs):
    import concourse.bacc as bacc
    from concourse.bass_utils import run_bass_kernel_spmd

    nc = bacc.Bacc("TRN2", target_bir_lowering=False, num_devices=1)
    arrays, I, O = {}, {}, {}
    for name in _INS:
        arrays[f"in_{name}"] = np.ascontiguousarray(inputs[name])
    arrays["in_consts"] = constants()
    for name in _INS + ["consts"]:
        a = arrays[f"in_{name}"]
        I[name] = nc.dram_tensor(f"in_{name}", a.shape, mybir.dt.from_np(a.dtype), kind="ExternalInput").ap()
    for name, shape in _OUTS.items():
        O[name] = nc.dram_tensor(f"out_{name}", shape, F32, kind="ExternalOutput").ap()
    build(nc, I, O)
    r = run_bass_kernel_spmd(nc, [arrays], core_ids=[0])
    return tuple(r.results[0][f"out_{name}"] for name in _OUTS)
```

```python
from contextlib import ExitStack

import numpy as np
import concourse.bass as bass
from concourse import mybir

F32 = mybir.dt.float32
BF16 = mybir.dt.bfloat16
I32 = mybir.dt.int32
ALU = mybir.AluOpType
ACT = mybir.ActivationFunctionType
AX_X = mybir.AxisListType.X
ds = bass.ds

P = 128
D = 1024
KD = D // P
SEQ = 512
NS = 8
NTOK = SEQ + NS
NT = 5
ROWS = [P, P, P, P, NS]
HALF = NTOK // 2
H = 4
QK = 64
VD = 128
POOL_W = (2, 4, 8, 16)
BUF = 15
PAD = 16
NE = 64
EF = 256
EPS = 1e-6
NCH = 12
ADA_ORDER = [2, 3, 0, 1, 8, 9, 4, 5, 6, 7, 10, 11]
FAR = 1024
ARENA = 53200
MAX_OVER = 32
NITEM = NE + MAX_OVER + 8
NO_SLOT = 640
NEG = -1.0e30

C_SIZES = dict(ident=P, psel=P, rope=NT * 2 * 2 * QK, dmat=H * P, qdec=2 * P, kdec=H, gam=4, icnt=4 * 16,
               tri=P, ones=P, iota=NO_SLOT + P, tok=NT * 3, before=64, rowok=NT,
               eye8=64, ecol=1, islot=40, bm=4, bmul=4)
C_AT, _at = {}, 0
for _n, _s in C_SIZES.items():
    C_AT[_n] = _at
    _at += _s
C_W = _at


def constants():
    c = np.zeros((P, C_W), np.float32)

    def put(name, value):
        value = np.asarray(value, np.float64)
        value = value.reshape(value.shape[0], -1)
        c[:value.shape[0], C_AT[name]:C_AT[name] + value.shape[1]] = value

    p = np.arange(P)
    put("ident", np.eye(P))
    pos = np.zeros((P, NT))
    for t in range(4):
        pos[:, t] = t * P + p
    pos[:, 4] = 4096.0
    freq = (np.float32(10000.0) ** (-np.arange(32, dtype=np.float32) / np.float32(32))).astype(np.float32)
    ang = (pos[:, :, None].astype(np.float32) * freq[None, None]).astype(np.float32).astype(np.float64)
    rope = np.zeros((P, NT, 2, 2, QK))
    for i, scale in enumerate((1.0, QK ** -0.5)):
        rope[:, :, 0, i, :32] = rope[:, :, 0, i, 32:] = np.cos(ang) * scale
        rope[:, :, 1, i, :32] = -np.sin(ang) * scale
        rope[:, :, 1, i, 32:] = np.sin(ang) * scale
    put("rope", rope)
    lg = np.log(1.0 - 2.0 ** (-5.0 - np.arange(H)))
    d = p[None, :] - p[:, None]
    put("dmat", np.stack([np.where(d >= 0, np.exp(lg[h] * np.maximum(d, 0)), 0.0) for h in range(H)], 1))
    qd = np.zeros((P, 2, P))
    gam = np.zeros((P, 2, 2))
    for pair in range(2):
        for half in range(2):
            rows = slice(64 * half, 64 * half + 64)
            qd[rows, pair] = np.exp(lg[2 * pair + half] * (p + 1.0))
            gam[rows, 0, pair] = np.exp(lg[2 * pair + half] * P)
            gam[rows, 1, pair] = np.exp(lg[2 * pair + half])
    put("qdec", qd)
    put("gam", gam)
    put("kdec", np.exp(lg[None, :] * (P - 1.0 - p)[:, None]))
    icnt = np.zeros((P, 4, 16))
    for g, w in enumerate(POOL_W):
        icnt[:, g] = 1.0 / np.minimum(np.arange(16) + 1.0, w)
    put("icnt", icnt)
    put("tri", p[:, None] < p[None, :])
    put("ones", np.ones((P, P)))
    put("iota", np.tile(np.arange(NO_SLOT + P), (P, 1)))
    tok = np.zeros((P, NT, 3))
    ids = np.arange(NT)[None] * P + p[:, None]
    tok[:, :, 0] = ids // 256 * 256 - FAR
    tok[:, :, 1] = ids % 256
    put("tok", tok)
    put("before", np.tile((np.arange(8)[None, :] < np.arange(8)[:, None]).reshape(1, 64), (P, 1)))
    put("rowok", (np.arange(NT)[None] * P + p[:, None]) < NTOK)
    put("eye8", np.tile(np.eye(8).reshape(1, 64), (P, 1)))
    put("psel", np.outer(p == NS, np.ones(P)))
    put("ecol", p[:, None])
    put("islot", np.tile(np.arange(40), (P, 1)))
    put("bm", np.tile(np.arange(4), (P, 1)))
    put("bmul", np.tile(128.0 * (np.arange(4) + 1), (P, 1)))
    return c


class Chain:

    def __init__(self, eng, sem, start=0):
        self.eng, self.sem, self.start, self.n = eng, sem, start, 0

    def do(self, ins):
        ins.then_inc(self.sem, 1)
        self.n += 1

    def settle(self):
        self.eng.wait_ge(self.sem, self.start + self.n)

    def link(self, ins):
        self.do(ins)
        self.settle()


def build(nc, I, O):
    ctx = ExitStack()
    with ctx:
        def sem(name):
            return ctx.enter_context(nc.semaphore(name))

        arena = ctx.enter_context(nc.sbuf_tensor("arena", [P, ARENA], F32))
        top = [0]

        def view(at, shape, dt=F32, rows=P):
            n = int(np.prod(shape))
            v = arena[0:rows, at:at + (n // 2 if dt == BF16 else n)]
            if dt != F32:
                v = v.bitcast(dt)
            if len(shape) == 2:
                v = v.rearrange("p (a b) -> p a b", b=shape[1])
            elif len(shape) == 3:
                v = v.rearrange("p (a b c) -> p a b c", b=shape[1], c=shape[2])
            elif len(shape) == 4:
                v = v.rearrange("p (a b c d) -> p a b c d", b=shape[1], c=shape[2], d=shape[3])
            return v

        def place(n):
            at = top[0]
            top[0] += n
            assert top[0] <= ARENA, top[0]
            return at

        CST = place(C_W)
        x_sb = view(place(NT * D), (NT, D))
        mod_at = place(6 * D)
        mod = view(mod_at, (6 * D,))
        bcA_at, bcB_at, bcG_at = place(D), place(D), place(D)
        bcA, bcB, bcG = (view(a, (D,)) for a in (bcA_at, bcB_at, bcG_at))
        hT_at = place(KD * NTOK)
        hT = view(hT_at, (KD, NTOK))
        hb_at = place(2 * D)
        hb = view(hb_at, (2, D))
        M = place(4 * NTOK + 4 * (PAD + NTOK) + 4 * NTOK + 8 * NTOK)
        W = place(18432)
        SM = place(64)
        csT_at = place(9 * KD)

        def const(name, n=None, rows=P):
            n = C_SIZES[name] if n is None else n
            return arena[0:rows, CST + C_AT[name]:CST + C_AT[name] + n]

        ident = const("ident")
        rope = const("rope").rearrange("p (t c q d) -> p t c q d", t=NT, c=2, q=2)
        dmat = const("dmat").rearrange("p (h i) -> p h i", h=H)
        qdec = const("qdec").rearrange("p (a i) -> p a i", a=2)
        gam = const("gam").rearrange("p (s a) -> p s a", s=2)
        icnt = const("icnt").rearrange("p (g n) -> p g n", g=4)
        iota = const("iota")
        tokc = const("tok").rearrange("p (t c) -> p t c", t=NT)

        ada_at = ([M, M + 4096, W, W + 4096] + 4 * [M + 8 * NTOK + 4 * (PAD + NTOK)] + 2 * [hT_at] + [W, W + 4096])
        ada = [view(a, (KD, 512)) for a in ada_at]
        gT = view(M, (4, NTOK))
        uT = view(M + 4 * NTOK, (4, PAD + NTOK))
        pT = view(M + 4 * NTOK + 4 * (PAD + NTOK), (4, NTOK))
        catT = view(M + 8 * NTOK + 4 * (PAD + NTOK), (8, NTOK))
        xg = view(M, (2, D))
        xgT = [view(M + 2048 + i * 1024, (KD, P)) for i in range(2)]
        sel = [view(M + 4096 + i * 640, (NT, P), BF16) for i in range(2)]
        act_sg = view(M + 5376, (2, EF))
        act_t = view(M + 5888, (2, EF))
        act_a = view(M + 6400, (2, EF))
        aT = view(M + 6912, (2, 2, P))
        Y = view(M + 7424, (2, D))
        w_qkv = view(W, (KD, 1024))
        w_gu = view(W + 8192, (KD, 1024))
        w_out = view(W, (KD, D))
        R0 = W + 8192
        v_sb = view(R0, (2, 512))
        qk_sb = view(R0 + 1024, (2, 512))
        rt = view(R0 + 2048, (2, 512))
        kd = view(R0 + 3072, (256,))
        qTz = view(R0 + 3328, (H, P))
        qTd = view(R0 + 3840, (H, P))
        kT = view(R0 + 4352, (2, P))
        scT = view(R0 + 4608, (H, P))
        St = view(R0 + 5120, (2, VD))
        on = view(R0 + 5376, (512,))
        w_pool = view(R0 + 5888, (4, P))
        pscale = view(R0 + 6400, (4,))
        S0 = view(W + 16384, (NS, 2, VD))
        nrm = view(W + 16384, (2, D), rows=9)
        pool_rows = [view(a, ((w - 1) * P,), rows=NS)
                     for a, w in zip((bcA_at + BUF * P, hb_at, bcG_at, bcA_at), POOL_W)]
        psum8 = view(hb_at + 1536, (512,), rows=NS)
        kd8 = view(M + 4 * NTOK, (NS, 256), rows=NS)
        qTm = view(hb_at, (H, 64))
        gu_w = [view(a, (KD, 512)) for a in (W, W + 4096, hT_at, mod_at)]
        dn_w = [view(W + 8192 + i * 2048, (2, D)) for i in range(4)]
        sh_gu = view(W + 12288, (KD, 512))
        sh_dn = view(W + 16384, (2, D))
        squares = view(M, (D,))
        wo_g = view(M + D, (2, 512))
        squares_end = view(M + 5376, (D,))
        yin = view(W, (NT, D))

        small = [SM]

        def tiny(shape, dt=F32, rows=P):
            at = small[0]
            small[0] += int(np.prod(shape))
            assert small[0] <= SM + 64
            return view(at, shape, dt, rows)

        csT = view(csT_at, (KD, 9))
        c_sb = view(hb_at, (D,), rows=9)
        c_sg = view(hb_at + D, (D,), rows=9)
        ss = tiny((8,))
        rstd = tiny((8,))
        bst = tiny((H, 6))
        mv = tiny((H, 2))
        lrs = tiny((H,))
        u8 = view(hb_at + 512, (512,), rows=NS)
        w_rt = view(W + 8192 + 3072, (KD, NE))
        small_route = W + 8192
        scores = view(small_route, (NT, NE))
        biased = view(small_route + 320, (NT, NE))
        rbias = view(small_route + 640, (NE,))
        top_a = view(small_route + 704, (40, 4))
        top_b = view(small_route + 864, (40, 4))
        top_c = view(small_route + 1024, (40, 2))
        top_d = view(small_route + 1104, (40, 2))
        top_e = view(small_route + 1184, (40, 2))
        top_f = view(small_route + 1264, (40, 2))
        gs = view(small_route + 1344, (NT, 8))
        rank = view(small_route + 1384, (NT, 8))
        cmp = view(small_route + 1424, (NT, 8, 8))
        cmp2 = view(small_route + 1744, (NT, 8, 8))
        v8 = view(small_route + 2064, (NT, 8))
        rep = view(small_route + 2104, (NT, NE))
        msk = view(small_route + 2424, (NT, NE), BF16)
        gsum = view(small_route + 2744, (8,))
        gates = rep
        gate_rest = biased
        over = view(small_route + 2752, (4, 40), rows=NE)
        ov_w = view(small_route + 2912, (2, 40), rows=NE)
        cnt = view(small_route + 2992, (4,), rows=NE)
        present = view(small_route + 3000, (4,), rows=NE)
        place_o = view(small_route + 3008, (4,), rows=NE)
        rt_at = CST + C_AT["rope"]
        posm = view(rt_at, (NT, NE))
        gate_parts = view(rt_at + 320, (NT, 3, NE), BF16)
        table = view(rt_at + 800, (2, NITEM), I32, rows=1)
        ones16 = view(rt_at + 1056, (P,), BF16)
        tri16 = view(rt_at + 1120, (P,), BF16)
        tablef = view(bcA_at, (2, NITEM), rows=1)
        nquad = view(rt_at + 800 + 2 * NITEM, (4,), I32, rows=1)
        info = [view(rt_at + 1012 + 16 * i, (NT, 6), BF16) for i in range(2)]
        gidx = view(rt_at + 1044, (2,), I32)
        sidx = view(rt_at + 1046, (2,), I32)
        got = view(rt_at + 1048, (2, 2))
        midx = view(rt_at + 1052, (2,), I32)
        mgate = view(rt_at + 1054, (2,))

        bank = [ctx.enter_context(nc.psum_tensor(f"bank{i}", [P, 512], F32)) for i in range(8)]

        h2_dram = nc.dram_tensor("h2_rows", (NTOK, D), F32).ap()
        sums = nc.dram_tensor("moe_sums", (NTOK, D), F32).ap()

        s_consts, s_ones = sem("other_constants_in"), sem("ones_made")
        s_const, s_c, s_nrm = sem("const_in"), sem("c_in"), sem("norms_in")
        s_x = [sem(f"x{t}_in") for t in range(NT)]
        s_ada, s_bada = [sem(f"ada_in{i}") for i in range(4)], sem("ada_bias_in")
        s_wgu, s_wqkv, s_wout = sem("w_gu_in"), sem("w_qkv_in"), sem("w_out_in")
        s_wpool, s_state, s_rows = sem("w_pool_in"), sem("state_in"), sem("pool_rows_in")
        s_rt, s_shw, s_nf = sem("router_in"), sem("shared_in"), sem("norm_f_in")
        s_sig_c, s_cs, s_csT, s_csTs = sem("c_sigmoid"), sem("c_silu"), sem("cT_done"), sem("cT_in_sbuf")
        s_adam, s_modv = sem("ada_products"), sem("mod_rows")
        s_ssq, s_var, s_std = sem("x_squares"), sem("x_var"), sem("x_std")
        s_bcm, s_bcs = sem("broadcast_products"), sem("broadcast_in_sbuf")
        s_hb, s_hTm, s_hTs = sem("h_rows"), sem("hT_done"), sem("hT_in_sbuf")
        s_gum, s_gsig, s_gv, s_uv = sem("gu_products"), sem("g_sigmoid"), sem("g_silu"), sem("u_in_sbuf")
        s_qkvm, s_vs, s_rot, s_kd = sem("qkv_products"), sem("v_in_sbuf"), sem("qk_rotated"), sem("k_decayed")
        s_qkT, s_kTs, s_qTz, s_qTd = sem("qkT_done"), sem("kT_in_sbuf"), sem("qT_in_sbuf"), sem("qT_decayed")
        s_scm, s_sc, s_o, s_stv = sem("scores_done"), sem("scores_decayed"), sem("o_done"), sem("state_updated")
        s_lv, s_ls, s_on, s_oT, s_cat = sem("o_var"), sem("o_std"), sem("o_normed"), sem("oT_done"), sem("cat_o")
        s_pad, s_pool, s_pm, s_pc = sem("pads"), sem("pooled"), sem("pool_products"), sem("cat_p")
        s_u8m, s_u8, s_ulm, s_ul = sem("u8_done"), sem("u8_in_sbuf"), sem("u_last_done"), sem("u_last_in_sbuf")
        s_p8, s_p8m, s_p8s = sem("p8_rows"), sem("p8T_done"), sem("p8T_in_sbuf")
        s_k8, s_qm, s_outer, s_snew = sem("k_spread"), sem("q_spread"), sem("outer_products"), sem("sample_states")
        s_zero = sem("zeros")
        s_store, s_h2st = sem("stores"), [sem(f"h2_rows_stored{i}") for i in range(2)]
        s_wo, s_x2, s_ssq2, s_var2, s_std2 = sem("out_products"), sem("x2"), sem("x2_squares"), sem("x2_var"), sem("x2_std")
        s_h2, s_h2T, s_h2Ts = sem("h2_rows_made"), sem("h2T_done"), sem("h2T_in_sbuf")
        s_rm, s_scr, s_msk, s_posm = sem("router_products"), sem("scores"), sem("chosen"), sem("slot_sums")
        s_ovx, s_ovm, s_ovw, s_tm, s_table = (sem(n) for n in ("extra_items", "extra_before", "extra_rows", "table_products", "table"))
        s_sel, s_selm, s_idx, s_sidx = sem("sel_ready"), sem("sel_done"), sem("idx_ready"), sem("scatter_idx")
        s_gat = [sem(f"gathered{i}") for i in range(2)]
        s_xT, s_xTs, s_gm, s_sg, s_a = sem("xT_done"), sem("xT_in_sbuf"), sem("gate_up_done"), sem("gate_sigmoid"), sem("a_ready")
        s_aT, s_aTs, s_dm, s_ya, s_yb = sem("aT_done"), sem("aT_in_sbuf"), sem("down_done"), sem("y_left"), sem("y_right")
        s_sca, s_ysh = sem("scattered"), [sem("shared_stored0"), sem("shared_stored1")]
        s_guw = [[sem(f"gate_up{i}_in{j}") for j in range(2)] for i in range(4)]
        s_gh = sem("gate_up_half")
        s_dnw = [sem(f"down_in{i}") for i in range(4)]
        s_yin = [sem(f"sums_in{i}") for i in range(NT)]
        s_x3, s_fs, s_fv, s_fsd, s_out = (sem(n) for n in ("x3", "x3_squares", "x3_var", "x3_std", "out_rows"))
        s_frs, s_xn, s_ost = sem("x3_rstd"), sem("x3_times_norm_f"), sem("out_stored")
        s_dp, s_dl, s_de = sem("vector_steps"), sem("vector_loop_steps"), sem("vector_end_steps")
        s_ap, s_pp = sem("scalar_steps"), sem("pool_steps")
        s_init, s_zero_q, s_rzero = sem("sums_set"), sem("q_zeros"), sem("scores_set")

        def tcols(t):
            return slice(t * P, t * P + ROWS[t])

        def bv(i, *dims, rows=P):
            n = int(np.prod(dims))
            v = bank[i][0:rows, 0:n]
            if len(dims) == 2:
                v = v.rearrange("p (a b) -> p a b", b=dims[1])
            elif len(dims) == 3:
                v = v.rearrange("p (a b c) -> p a b c", b=dims[1], c=dims[2])
            return v

        def wait_y_free(eng, n, before):
            if before is not None:
                eng.wait_ge(s_sca, before * 16 + 16)
            elif n >= 2:
                eng.wait_ge(s_ysh[n % 2], 16 * ((n - 2) // 2 + 1))

        H1_BANKS = ((4, 5), (6, 0))
        ADA_BANK = (1, 2, 1, 2, 3, 7, 3, 7, 3, 7, 4, 5)

        def seg(n, rows):
            return mod[0:rows, n * D:(n + 1) * D]

        blk = ctx.enter_context(nc.Block())

        @blk.sync
        def _(sp):
            sp.dma_start(c_sb[0:NS, :], I["c_sample"]).then_inc(s_c, 16)
            sp.dma_start(c_sb[NS:NS + 1, :], I["c_prompt"]).then_inc(s_c, 16)
            sp.dma_start(arena[:, CST:CST + 2 * P], I["consts"][:, 0:2 * P]).then_inc(s_const, 16)
            wa = I["w_ada"][0].rearrange("(p k) n -> p k n", k=KD)
            wi = I["w_in"][0].rearrange("(p k) n -> p k n", k=KD)

            def load_ada(c):
                at = ADA_ORDER[c] * 512
                sp.dma_start(ada[c], wa[:, :, at:at + 512]).then_inc(s_ada[c % 4], 16)

            load_ada(0)
            sp.dma_start(mod[0:9, :], I["b_ada"][0].partition_broadcast(9)).then_inc(s_bada, 16)
            sp.dma_start(nrm[:, 0, :], I["norm1"][0].partition_broadcast(9)).then_inc(s_nrm, 16)
            sp.dma_start(nrm[:, 1, :], I["norm2"][0].partition_broadcast(9)).then_inc(s_nrm, 16)
            for c in range(1, 4):
                load_ada(c)
            for t in range(4):
                sp.dma_start(x_sb[:, t, :], I["x_prompt"][0, t * P:(t + 1) * P, :]).then_inc(s_x[t], 16)
            sp.dma_start(x_sb[0:NS, 4, :], I["x_sample"].rearrange("b s d -> (b s) d")).then_inc(s_x[4], 16)
            sp.dma_start(w_gu, wi[:, :, 1024:2048]).then_inc(s_wgu, 16)
            sp.wait_ge(s_adam, 2)
            load_ada(4)
            sp.dma_start(arena[:, CST + 2 * P:CST + C_W], I["consts"][:, 2 * P:]).then_inc(s_consts, 16)
            sp.wait_ge(s_adam, 4)
            sp.dma_start(w_qkv, wi[:, :, 0:1024]).then_inc(s_wqkv, 16)
            sp.wait_ge(s_hb, NT)
            sp.wait_ge(s_hTm, NT)
            pool_in = I["state_pool"][0]
            for g, w in enumerate(POOL_W):
                sp.dma_start(pool_rows[g].rearrange("p (r c) -> p r c", c=P),
                             pool_in[:, BUF - w + 1:BUF, g * P:(g + 1) * P]).then_inc(s_rows, 16)
            sp.wait_ge(s_adam, 5)
            load_ada(5)
            sp.dma_start(O["pool_s"][0, :, 0:BUF - 1, :], pool_in[:, 1:BUF, :]).then_inc(s_store, 16)
            sp.wait_ge(s_adam, 6)
            load_ada(6)
            sp.wait_ge(s_modv, 6)
            for a in range(2):
                src = I["state_ret"][0].rearrange("s (a b) d v -> a b d s v", b=2)
                for b in range(2):
                    sp.dma_start(S0[64 * b:64 * b + 64, :, a, :], src[a, b]).then_inc(s_state, 16)
            sp.wait_ge(s_adam, 7)
            load_ada(7)
            sp.wait_ge(s_gum, 16)
            sp.dma_start(w_pool, I["w_pool"][0].rearrange("g c d -> c g d")).then_inc(s_wpool, 16)
            with nc.allow_non_contiguous_dma(reason="512 numbers, once"):
                sp.dma_start(pscale, I["pool_scale"][0].rearrange("(g p) -> p g", p=P)).then_inc(s_wpool, 16)
            sp.wait_ge(s_u8, 1)
            sp.dma_start(O["pool_s"][0, :, BUF - 1, :], u8).then_inc(s_store, 16)
            sp.wait_ge(s_ul, 1)
            sp.dma_start(O["pool_p"][0, 0], hb[0:BUF, 1, 0:512]).then_inc(s_store, 16)
            sp.wait_ge(s_qkvm, NT)
            load_ada(8)
            sp.dma_start(w_out, I["w_out"][0].rearrange("(k p) n -> p k n", p=P)).then_inc(s_wout, 16)
            sp.wait_ge(s_adam, 9)
            load_ada(9)
            sp.wait_ge(s_stv, 16)
            sp.dma_start(O["ret_p"][0, 0].rearrange("(a b) d v -> (b d) a v", b=2), St).then_inc(s_store, 16)
            sp.wait_ge(s_snew, 16)
            for a in range(2):
                dst = O["ret_s"][0].rearrange("s (a b) d v -> a b d s v", b=2)
                for b in range(2):
                    sp.dma_start(dst[a, b], S0[64 * b:64 * b + 64, :, a, :]).then_inc(s_store, 16)
            sp.wait_ge(s_cat, NT)
            sp.wait_ge(s_pm, 8)
            sp.wait_ge(s_pc, 8)
            sp.wait_ge(s_outer, 8)
            sp.wait_ge(s_o, NT)
            sp.wait_ge(s_store, 16 * 8)
            sp.dma_start(w_rt, I["w_router"][0].rearrange("(p k) e -> p k e", k=KD)).then_inc(s_rt, 16)
            for i, name in enumerate(("w_sh_gate", "w_sh_up")):
                sp.dma_start(sh_gu[:, :, i * EF:(i + 1) * EF],
                             I[name][0].rearrange("(p k) f -> p k f", k=KD)).then_inc(s_shw, 16)
            sp.dma_start(sh_dn, I["w_sh_down"][0].rearrange("(p k) n -> p k n", k=2)).then_inc(s_shw, 16)
            for t in range(NT):
                sp.wait_ge(s_h2, t + 1)
                sp.dma_start(h2_dram[t * P:t * P + ROWS[t], :], hb[0:ROWS[t], t % 2, :]).then_inc(s_h2st[t % 2], 16)
                if t == 2:
                    sp.wait_ge(s_wo, NT)
                    load_ada(10)
                    load_ada(11)

            eg = [I[n][0].rearrange("e (p k) f -> p e k f", k=KD) for n in ("w_exp_gate", "w_exp_up")]
            ed = I["w_exp_down"][0].rearrange("e (p k) n -> p e k n", k=2)

            def load_gate_up(e, q, half):
                k = slice(4 * half, 4 * half + 4)
                for i in range(2):
                    sp.dma_start(gu_w[q][:, k, i * EF:(i + 1) * EF].unsqueeze(1),
                                 eg[i][:, ds(e, 1), k]).then_inc(s_guw[q][half], 16)

            def load_down(e, q):
                sp.dma_start(dn_w[q].unsqueeze(1), ed[:, ds(e, 1)]).then_inc(s_dnw[q], 16)

            def load_item(w, e, q):
                for half in range(2):
                    sp.wait_ge(s_gm if half else s_gh, w - 4 + NT + 1)
                    load_gate_up(e, q, half)
                sp.wait_ge(s_dm, w - 4 + NT + 1)
                load_down(e, q)

            def store_shared(n):
                sp.wait_ge(s_ya, n + 1)
                sp.wait_ge(s_yb, n + 1)
                sp.dma_start(sums[n * P:n * P + ROWS[n], :], Y[0:ROWS[n], n % 2, :]).then_inc(s_ysh[n % 2], 16)

            sp.wait_ge(s_adam, NCH)
            for w in range(2):
                for half in range(2):
                    load_gate_up(w, w, half)
            store_shared(0)
            sp.wait_ge(s_h2, NT)
            sp.wait_ge(s_bcs, 10)
            for half in range(2):
                load_gate_up(3, 3, half)
            store_shared(1)
            sp.wait_ge(s_table, 1)
            store_shared(2)
            for w in range(2):
                load_down(w, w)
            sp.wait_ge(s_gm, NT)
            for half in range(2):
                load_gate_up(2, 2, half)
            store_shared(3)
            load_down(2, 2)
            load_down(3, 3)
            store_shared(4)
            sp.dma_start(bcA, I["norm_f"].partition_broadcast(P)).then_inc(s_nf, 16)
            with sp.Fori(1, NE // 4) as i:
                for q in range(4):
                    load_item(i * 4 + q, i * 4 + q, q)
            sp.wait_ge(s_table, 1)
            more = sp.value_load(nquad[0:1, 0:1], min_val=NE // 4 - 1, max_val=(NE + MAX_OVER - 1) // 4)
            with sp.Fori(NE // 4, more + 1) as i:
                for q in range(4):
                    e = sp.value_load(table[0:1, 0, ds(i * 4 + q, 1)], min_val=0, max_val=NE - 1)
                    load_item(i * 4 + q, e, q)
            sp.wait_ge(s_ya, more * 4 + (NT + 4))
            sp.wait_ge(s_yb, more * 4 + (NT + 4))
            sp.wait_ge(s_sca, more * 64 + 80)
            for t in range(NT):
                sp.dma_start(yin[0:ROWS[t], t, :], sums[t * P:t * P + ROWS[t], :]).then_inc(s_yin[t], 16)
            for t in range(NT):
                sp.wait_ge(s_out, t + 1)
                dst = O["y_p"][0, t * P:(t + 1) * P, :] if t < 4 else O["y_s"].rearrange("b s d -> (b s) d")
                sp.dma_start(dst, yin[0:ROWS[t], t, :]).then_inc(s_ost, 16)
            sp.wait_ge(s_ost, 16 * NT)
            sp.wait_ge(s_store, 16 * 8)

        @blk.gpsimd
        def _(pool):
            ch = Chain(pool, s_pp)
            pool.wait_ge(s_adam, 2)
            for g in range(4):
                ins = pool.memset(uT[:, g, 0:PAD], 0.0)
            ins.then_inc(s_pad, 1)
            L = PAD + SEQ
            wa = view(M + 8 * NTOK + 4 * (PAD + NTOK) + 4 * NTOK, (L,))
            wb = view(M + 8 * NTOK + 4 * (PAD + NTOK) + 5 * NTOK + 2 * PAD, (L,))
            pool.wait_ge(s_pad, 1)
            pool.wait_ge(s_consts, 16)
            pool.wait_ge(s_uv, 8)
            pool.wait_ge(s_adam, 8)
            for g, w in enumerate(POOL_W):
                u = uT[:, g, :]
                src, step = u, 1
                for b in [wa, wb, wa, wb][:g + 1]:
                    ch.link(pool.tensor_tensor(b[:, 2 * step - 1:L], src[:, 2 * step - 1:L], src[:, step - 1:L - step], ALU.add))
                    src, step = b, step * 2
                ch.do(pool.tensor_scalar(pT[:, g, 16:SEQ], src[:, PAD + 16:L], 1.0 / w, None, ALU.mult))
                ch.link(pool.tensor_tensor(pT[:, g, 0:16], src[:, PAD:PAD + 16], icnt[:, g, :], ALU.mult))
                last = pool.tensor_tensor(pT[:, g, 0:SEQ], pT[:, g, 0:SEQ], u[:, PAD:L], ALU.subtract)
                last.then_inc(s_pool, 1)
                pool.wait_ge(s_pool, g + 1)
            pool.wait_ge(s_wo, NT)
            pool.wait_ge(s_x2, 2 * NT)
            pool.wait_ge(s_ssq2, NT)
            pool.memset(xg, 0.0).then_inc(s_zero, 1)
            pool.dma_start(rbias, I["router_bias"][0].partition_broadcast(P)).then_inc(s_sca, 16)
            pool.wait_ge(s_zero, 1)
            pool.wait_ge(s_sca, 16)

            zero_reg, bound = pool.alloc_register("from_zero"), pool.alloc_register("row_bound")
            pool.reg_mov(zero_reg, 0)

            def gather(w, par):
                pool.wait_ge(s_idx, w + 1)
                if not (isinstance(w, int) and w < 2):
                    pool.wait_ge(s_xT, w - 1)
                pool.wait_ge(s_h2st[0], 48)
                pool.wait_ge(s_h2st[1], 32)
                pool.reg_add(bound, zero_reg, NTOK - 1)
                pool.indirect_dma_start(out=xg[:, par, :], out_offset=None, in_=h2_dram,
                                        in_offset=bass.IndirectOffsetOnAxis(ap=gidx[:, par:par + 1], axis=0),
                                        bounds_check=bound, oob_is_err=False).then_inc(s_gat[par], 16)

            def scatter(w, par):
                pool.wait_ge(s_sidx, w + 1)
                pool.wait_ge(s_ya, w + NT + 1)
                pool.wait_ge(s_yb, w + NT + 1)
                pool.wait_ge(s_sca, w * 16 + 16)
                pool.wait_ge(s_ysh[0], 16 * 3)
                pool.wait_ge(s_ysh[1], 16 * 2)
                pool.reg_add(bound, zero_reg, NTOK - 1)
                pool.indirect_dma_start(out=sums, out_offset=bass.IndirectOffsetOnAxis(ap=sidx[:, par:par + 1], axis=0),
                                        in_=Y[:, (par + NT) % 2, :], in_offset=None,
                                        bounds_check=bound, oob_is_err=False,
                                        compute_op=ALU.add).then_inc(s_sca, 16)

            gather(0, 0)
            gather(1, 1)
            gather(2, 0)
            gather(3, 1)
            scatter(0, 0)
            gather(4, 0)
            scatter(1, 1)
            gather(5, 1)
            scatter(2, 0)
            pool.wait_ge(s_table, 1)
            more = pool.value_load(nquad[0:1, 0:1], min_val=NE // 4 - 1, max_val=(NE + MAX_OVER - 1) // 4)
            with pool.Fori(1, more + 1) as i:
                for j in range(4):
                    gather(i * 4 + (2 + j), j % 2)
                    scatter(i * 4 + (j - 1), 1 - j % 2)
            scatter(more * 4 + 3, 1)
            for par in range(2):
                pool.wait_ge(s_gat[par], more * 32 + 48)
            pool.wait_ge(s_sca, more * 64 + 80)
            pool.wait_ge(s_nf, 16)
            for t in range(NT):
                R = ROWS[t]
                pool.wait_ge(s_x3, t + 1)
                pool.tensor_tensor(yin[0:R, t, :], x_sb[0:R, t, :], bcA[0:R, :], ALU.mult).then_inc(s_xn, 1)

        @blk.tensor
        def _(pe):
            mm = pe.matmul
            pe.wait_ge(s_const, 16)
            pe.wait_ge(s_cs, 1)
            cv = c_sb.rearrange("p (q k) -> p k q", k=KD)
            for k in range(KD):
                ins = pe.transpose(bank[0][:, k * 9:(k + 1) * 9], cv[:, k, :], ident[0:9, 0:9])
            ins.then_inc(s_csT, 1)
            pe.wait_ge(s_csTs, 1)

            def ada_rows(c):
                pe.wait_ge(s_ada[c % 4], 16 * (c // 4 + 1))
                if c >= 2:
                    pe.wait_ge(s_modv, c - 1)
                for h in range(2):
                    for j in range(4):
                        k = 2 * j + h
                        ins = mm(bank[ADA_BANK[c]][32 * j:32 * j + 9, :], csT[:, k, :], ada[c][:, k, :],
                                 start=(h == 0), stop=(h == 1), tile_position=(0, 32 * j))
                ins.then_inc(s_adam, 1)

            def sample_product(b, left, right, n, k, last):
                for j in range(4):
                    ins = mm(bank[b][32 * j:32 * j + NS, 0:n], left, right[:, k, j * n:(j + 1) * n],
                             start=(k == 0), stop=(k == last), tile_position=(0, 32 * j))
                return ins

            def broadcast(n, i):
                for f in range(2):
                    if 0 < i < 5:
                        pe.wait_ge(s_bcs, 2 * (i - 1) + f + 1)
                    mm(bank[(3, 7)[f] if i < 5 else 4 + f][:, :], const("psel", rows=9), seg(n, 9)[:, f * 512:(f + 1) * 512],
                       start=True, stop=True).then_inc(s_bcm, 1)

            for c in range(3):
                ada_rows(c)
            pe.wait_ge(s_modv, 2)
            broadcast(1, 0)
            ada_rows(3)
            pe.wait_ge(s_modv, 4)
            broadcast(0, 1)

            def transposes(src, rows, banks, done):
                sv = src.rearrange("p (q k) -> p k q", k=KD)
                for k in range(KD):
                    b = bv(banks[k // 4], 4, rows)
                    ins = pe.transpose(b[:, k % 4, :], sv[:, k, :], ident[0:rows, 0:rows])
                ins.then_inc(done, 1)

            for t in range(NT):
                pe.wait_ge(s_hb, t + 1)
                if t >= 2:
                    pe.wait_ge(s_hTs, t - 1)
                transposes(hb[0:ROWS[t], t % 2, :], ROWS[t], H1_BANKS[t % 2], s_hTm)
            pe.wait_ge(s_bcs, 4)
            pe.wait_ge(s_hTs, NT)
            pe.wait_ge(s_wgu, 16)
            GB = (0, 1, 2, 6)
            for i in range(16):
                n, f = i // 2, i % 2
                if 4 <= i < 12:
                    pe.wait_ge(s_gv, i - 3)
                elif i >= 12:
                    pe.wait_ge(s_uv, i - 11)
                for k in range(KD):
                    ins = mm(bank[GB[i % 4]][:, 0:HALF], w_gu[:, k, n * P:(n + 1) * P],
                             hT[:, k, f * HALF:(f + 1) * HALF], start=(k == 0), stop=(k == KD - 1))
                ins.then_inc(s_gum, 1)
                if i in (1, 5, 9, 13):
                    ada_rows(4 + i // 4)

            def qkv(t, part):
                if part == 0:
                    if t == 0:
                        pe.wait_ge(s_wqkv, 16)
                        pe.wait_ge(s_uv, 8)
                        pe.wait_ge(s_bcs, 4)
                    if t >= 2:
                        pe.wait_ge(s_rot, t - 1)
                        pe.wait_ge(s_vs, t - 1)
                b = 2 * (t % 2)
                R = ROWS[t]
                for k in (2 * part, 2 * part + 1):
                    if t == 4:
                        ins = sample_product(b, hT[:, k, tcols(4)], w_qkv, 256, k, KD - 1)
                    for f in range(2 if t < 4 else 0):
                        ins = mm(bank[b + f][0:R, :], hT[:, k, tcols(t)], w_qkv[:, k, f * 512:(f + 1) * 512],
                                 start=(k == 0), stop=(k == KD - 1))
                if part == 3:
                    ins.then_inc(s_qkvm, 1)

            def qk_transposes(t):
                R = ROWS[t]
                pe.wait_ge(s_rot, t + 1)
                if t >= 1:
                    pe.wait_ge(s_cat, t)
                else:
                    pe.wait_ge(s_u8, 1)
                b = bv(4, 4, R)
                for j in range(4):
                    ins = pe.transpose(b[:, j, :], qk_sb[0:R, t % 2, j * P:(j + 1) * P], ident[0:R, 0:R])
                ins.then_inc(s_qkT, 1)

            def retention_scores(t):
                pe.wait_ge(s_kTs, t + 1)
                pe.wait_ge(s_qTz, t + 1)
                pe.wait_ge(s_ul, 1)
                for h in range(H):
                    ins = mm(bank[5][:, h * P:(h + 1) * P], kT[:, h // 2, :], qTz[:, h, :], start=True, stop=True)
                ins.then_inc(s_scm, 1)

            def retention_out(t):
                pe.wait_ge(s_sc, t + 1)
                pe.wait_ge(s_vs, t + 1)
                pe.wait_ge(s_qTd, t + 1)
                if t >= 1:
                    pe.wait_ge(s_stv, 4 * t)
                    pe.wait_ge(s_on, t)
                for h in range(H):
                    o = bank[6][:, h * P:(h + 1) * P]
                    mm(o, scT[:, h, :], v_sb[:, t % 2, h * P:(h + 1) * P], start=True, stop=(t == 0))
                    if t >= 1:
                        ins = mm(o, qTd[:, h, :], St[:, h // 2, :], start=False, stop=True)
                pe.wait_ge(s_kd, t + 1)
                pe.wait_ge(s_p8s, 1)
                for a in range(2):
                    ins = mm(bank[7][:, a * 256:(a + 1) * 256], kd[:, a * P:(a + 1) * P],
                             v_sb[:, t % 2, a * 256:(a + 1) * 256], start=True, stop=True)
                ins.then_inc(s_o, 1)

            def o_transposes(t):
                R = ROWS[t]
                pe.wait_ge(s_on, t + 1)
                b = bv(4, 4, R)
                for h in range(H):
                    ins = pe.transpose(b[:, h, :], on[0:R, h * P:(h + 1) * P], ident[0:R, 0:R])
                ins.then_inc(s_oT, 1)

            qkv(0, 0)
            for g in range(4):
                ins = pe.transpose(bank[4][0:NS, g * P:(g + 1) * P], uT[:, g, PAD + SEQ:PAD + NTOK], ident)
            ins.then_inc(s_u8m, 1)
            for g in range(4):
                ins = pe.transpose(bank[5][0:BUF, g * P:(g + 1) * P], uT[:, g, PAD + SEQ - BUF:PAD + SEQ], ident)
            ins.then_inc(s_ulm, 1)
            for part in range(1, 4):
                qkv(0, part)
            pe.wait_ge(s_p8, 1)
            pe.wait_ge(s_modv, 8)
            b = bv(7, 4, NS)
            for g in range(4):
                ins = pe.transpose(b[:, g, :], psum8[:, g * P:(g + 1) * P], ident[0:NS, 0:NS])
            ins.then_inc(s_p8m, 1)
            def outer(i):
                a, s2 = i // 4, i % 4
                if i == 0:
                    pe.wait_ge(s_k8, 1)
                    pe.wait_ge(s_rot, 5)
                    pe.wait_ge(s_vs, 5)
                if i >= 2:
                    pe.wait_ge(s_snew, 2 * (i - 1))
                for j in range(2):
                    s = 2 * s2 + j
                    ins = mm(bank[i % 2][:, j * 256:(j + 1) * 256], kd8[:, s, a * P:(a + 1) * P],
                             v_sb[0:NS, 0, a * 256:(a + 1) * 256], start=True, stop=True)
                ins.then_inc(s_outer, 1)

            def pool_product(i):
                g, f = i // 2, i % 2
                if i == 0:
                    pe.wait_ge(s_p8s, 1)
                    pe.wait_ge(s_pool, 4)
                    pe.wait_ge(s_wpool, 32)
                    pe.wait_ge(s_rot, 4)
                    pe.wait_ge(s_sc, 4)
                if i >= 2:
                    pe.wait_ge(s_pc, i - 1)
                mm(bank[(2, 5)[i % 2]][:, 0:HALF], w_pool[:, g, :], pT[:, g, f * HALF:(f + 1) * HALF],
                   start=True, stop=True).then_inc(s_pm, 1)

            for t in range(4):
                qkv(t + 1, 0)
                qk_transposes(t)
                qkv(t + 1, 1)
                retention_scores(t)
                qkv(t + 1, 2)
                if t == 3:
                    qkv(4, 3)
                retention_out(t)
                if t < 3:
                    qkv(t + 1, 3)
                    o_transposes(t)
            outer(0)
            outer(1)
            pool_product(0)
            pool_product(1)
            pe.wait_ge(s_vs, 4)
            pe.wait_ge(s_stv, 16)
            broadcast(2, 2)
            broadcast(4, 3)
            o_transposes(3)
            for i in (2, 3):
                pool_product(i)
                outer(i)
            pe.wait_ge(s_bcs, 8)
            ada_rows(8)
            qk_transposes(4)
            for i in range(4, 8):
                pool_product(i)
                outer(i)
            ada_rows(9)
            pe.wait_ge(s_snew, 16)
            pe.wait_ge(s_qm, 1)
            pe.wait_ge(s_on, 4)
            for h in range(H):
                for s in range(NS):
                    ins = mm(bank[6][0:NS, h * P:(h + 1) * P], qTm[:, h, s * 8:(s + 1) * 8], S0[:, s, h // 2, :],
                             start=(s == 0), stop=(s == NS - 1))
            ins.then_inc(s_o, 1)
            pe.wait_ge(s_modv, 10)
            broadcast(3, 4)
            o_transposes(4)

            def out_tile(t):
                b = 2 * ((t + 1) % 2)
                R = ROWS[t]
                if t >= 2:
                    pe.wait_ge(s_x2, 2 * (t - 1))
                for k in range(KD):
                    if t == 4:
                        ins = sample_product(b, catT[:, k, tcols(4)], w_out, 256, k, KD - 1)
                    for f in range(2 if t < 4 else 0):
                        ins = mm(bank[b + f][0:R, :], catT[:, k, tcols(t)], w_out[:, k, f * 512:(f + 1) * 512],
                                 start=(k == 0), stop=(k == KD - 1))
                ins.then_inc(s_wo, 1)

            def h2_tile(t):
                R = ROWS[t]
                pe.wait_ge(s_h2, t + 1)
                if t >= 1:
                    pe.wait_ge(s_h2Ts, t)
                transposes(hb[0:R, t % 2, :], R, (4, 5), s_h2T)

            pe.wait_ge(s_pc, 8)
            pe.wait_ge(s_bcs, 10)
            pe.wait_ge(s_wout, 16)
            pe.wait_ge(s_cat, NT)
            out_tile(0)
            out_tile(1)
            h2_tile(0)
            out_tile(2)
            h2_tile(1)
            out_tile(3)
            h2_tile(2)
            out_tile(4)

            def gate_up(n, xT, wts, R, gb, part):
                for k in range(4 * part, 4 * part + 4):
                    if R == NS:
                        ins = sample_product(gb, xT[k], wts, P, k, KD - 1)
                        continue
                    ins = mm(bank[gb][0:R, :], xT[k], wts[:, k, :], start=(k == 0), stop=(k == KD - 1))
                ins.then_inc(s_gm if part else s_gh, 1)

            def a_transposes(n, R, par):
                pe.wait_ge(s_a, n + 1)
                if not (isinstance(n, int) and n == 0):
                    pe.wait_ge(s_aTs, n)
                av = act_a[0:R, par, :].rearrange("p (q k) -> p k q", k=2)
                for k in range(2):
                    ins = pe.transpose(bank[6][:, k * P:k * P + R], av[:, k, :], ident[0:R, 0:R])
                ins.then_inc(s_aT, 1)

            def down(n, R, par, wts):
                pe.wait_ge(s_aTs, n + 1)
                if not (isinstance(n, int) and n == 0):
                    pe.wait_ge(s_ya, n)
                    pe.wait_ge(s_yb, n)
                if R == NS:
                    for k in range(2):
                        ins = sample_product(2, aT[:, par, k, 0:NS], wts, 256, k, 1)
                for f in range(2 if R > NS else 0):
                    for k in range(2):
                        ins = mm(bank[2 + f][0:R, :], aT[:, par, k, 0:R], wts[:, k, f * 512:(f + 1) * 512],
                                 start=(k == 0), stop=(k == 1))
                ins.then_inc(s_dm, 1)

            def shared_gu(n, part):
                if part == 0:
                    pe.wait_ge(s_h2Ts, n + 1)
                    if n == 0:
                        pe.wait_ge(s_shw, 48)
                        pe.wait_ge(s_x2, 8)
                    if n >= 2:
                        pe.wait_ge(s_a, n - 1)
                gate_up(n, [hT[:, k, tcols(n)] for k in range(KD)], sh_gu, ROWS[n], n % 2, part)

            shared_gu(0, 0)
            h2_tile(3)
            shared_gu(0, 1)
            h2_tile(4)
            shared_gu(1, 0)
            pe.wait_ge(s_h2Ts, NT)
            pe.wait_ge(s_rt, 16)
            for t in range(NT):
                for k in range(KD):
                    ins = mm(bank[6][0:ROWS[t], t * NE:(t + 1) * NE], hT[:, k, tcols(t)], w_rt[:, k, :],
                             start=(k == 0), stop=(k == KD - 1))
            ins.then_inc(s_rm, 1)
            ada_rows(10)
            ada_rows(11)
            shared_gu(1, 1)
            pe.wait_ge(s_msk, 1)
            pe.wait_ge(s_ones, 1)
            for t in range(NT):
                for j in range(t + 1):
                    ins = mm(bank[7][:, t * NE:(t + 1) * NE], ones16 if j < t else tri16, msk[:, j, :],
                             start=(j == 0), stop=(j == t))
            for t in range(NT):
                ins = mm(bank[7][0:NE, 320:321], msk[:, t, :], ones16[:, 0:1], start=(t == 0), stop=(t == NT - 1))
            ins.then_inc(s_posm, 1)
            pe.wait_ge(s_scr, NT)
            a_transposes(0, ROWS[0], 0)
            pe.wait_ge(s_x2, 10)
            down(0, ROWS[0], 0, sh_dn)
            shared_gu(2, 0)
            shared_gu(2, 1)
            pe.wait_ge(s_ovx, 1)
            mm(bank[7][0:NE, 384:385], const("tri", NE, rows=NE), cnt[:, 1:2], start=True, stop=True).then_inc(s_ovm, 1)
            a_transposes(1, ROWS[1], 1)
            down(1, ROWS[1], 1, sh_dn)
            shared_gu(3, 0)
            pe.wait_ge(s_ovw, 1)
            mm(bank[7][0:1, 388:428], const("ecol", rows=NE), ov_w[:, 0, :], start=True, stop=True)
            mm(bank[7][0:1, 428:468], const("ones", 1, rows=NE), ov_w[:, 1, :], start=True, stop=True)
            mm(bank[7][0:1, 468:469], cnt[:, 1:2], const("ones", 1, rows=NE), start=True, stop=True).then_inc(s_tm, 1)
            shared_gu(3, 1)

            def select(w, par):
                pe.wait_ge(s_sel, w + 1)
                if isinstance(w, int) and w == 0:
                    pe.wait_ge(s_table, 1)
                else:
                    pe.wait_ge(s_idx, w)
                for t in range(NT):
                    ins = mm(bank[7][:, 0:6], sel[par][:, t, :], info[par][:, t, :], start=(t == 0), stop=(t == NT - 1))
                ins.then_inc(s_selm, 1)

            def x_transposes(w, par):
                pe.wait_ge(s_gat[par], (w - par) * 8 + 16)
                if not (isinstance(w, int) and w == 0):
                    pe.wait_ge(s_xTs, w)
                transposes(xg[:, par, :], P, (4, 5), s_xT)

            def item(w, q, first=False):
                n, par = w + NT, q % 2
                pe.wait_ge(s_xTs, w + 1)
                pe.wait_ge(s_guw[q][0], (w - q) * 8 + 32)
                pe.wait_ge(s_a, n - 1)
                xT = [xgT[par][:, k, :] for k in range(KD)]
                gate_up(n, xT, gu_w[q], P, (par + NT) % 2, 0)
                select(w + 2, par)
                R = ROWS[4] if first else P
                a_transposes(n - 1, R, (par + NT - 1) % 2)
                pe.wait_ge(s_guw[q][1], (w - q) * 8 + 32)
                gate_up(n, xT, gu_w[q], P, (par + NT) % 2, 1)
                x_transposes(w + 1, 1 - par)
                if first:
                    down(n - 1, R, (par + NT - 1) % 2, sh_dn)
                else:
                    qb = (q - 1) % 4
                    pe.wait_ge(s_dnw[qb], w * 4 + (12 - 4 * qb))
                    down(n - 1, R, (par + NT - 1) % 2, dn_w[qb])

            a_transposes(2, P, 0)
            down(2, P, 0, sh_dn)
            select(0, 0)
            shared_gu(4, 0)
            a_transposes(3, P, 1)
            shared_gu(4, 1)
            down(3, P, 1, sh_dn)
            select(1, 1)
            pe.wait_ge(s_modv, NCH)
            broadcast(5, 5)
            pe.wait_ge(s_bcs, 12)
            x_transposes(0, 0)
            item(0, 0, first=True)
            for w in range(1, 4):
                item(w, w)
            pe.wait_ge(s_table, 1)
            more = pe.value_load(nquad[0:1, 0:1], min_val=NE // 4 - 1, max_val=(NE + MAX_OVER - 1) // 4)
            with pe.Fori(1, more + 1) as i:
                for q in range(4):
                    item(i * 4 + q, q)
            a_transposes(more * 4 + (NT + 3), P, 0)
            pe.wait_ge(s_dnw[3], more * 16 + 16)
            down(more * 4 + (NT + 3), P, 0, dn_w[3])

        @blk.scalar
        def _(act):
            A = nc.scalar.activation
            ch = Chain(act, s_ap)
            act.wait_ge(s_c, 32)
            A(c_sg, c_sb, ACT.Sigmoid).then_inc(s_sig_c, 1)
            act.wait_ge(s_csT, 1)
            A(csT.rearrange("p k c -> p (k c)"), bank[0][:, 0:72], ACT.Copy).then_inc(s_csTs, 1)
            def broadcast_copies(i, dst):
                for f in range(2):
                    act.wait_ge(s_bcm, 2 * i + f + 1)
                    A(dst[:, f * 512:(f + 1) * 512], bank[(3, 7)[f] if i < 5 else 4 + f][:, :], ACT.Copy).then_inc(s_bcs, 1)

            broadcast_copies(0, bcA)
            act.wait_ge(s_init, 1)
            for t in range(NT):
                act.wait_ge(s_x[t], 16)
                A(hT.rearrange("p k n -> p (k n)")[0:ROWS[t], 0:D], x_sb[0:ROWS[t], t, :], ACT.Square,
                  accum_out=ss[0:ROWS[t], t:t + 1]).then_inc(s_ssq, 1)
                act.wait_ge(s_ssq, t + 1)
            act.wait_ge(s_var, 1)
            A(rstd[:, 0:NT], rstd[:, 0:NT], ACT.Sqrt).then_inc(s_std, 1)

            broadcast_copies(1, bcB)

            def hT_copies(R, t, done, dm, banks=(4, 5)):
                act.wait_ge(dm, t + 1)
                for i in range(2):
                    ins = A(hT[:, 4 * i:4 * i + 4, tcols(t)], bv(banks[i], 4, R), ACT.Copy)
                    ch.do(ins) if i == 0 else ins.then_inc(done, 1)

            for t in range(NT):
                hT_copies(ROWS[t], t, s_hTs, s_hTm, H1_BANKS[t % 2])
            for i in range(16):
                n, f = i // 2, i % 2
                act.wait_ge(s_gum, i + 1)
                b = bank[(0, 1, 2, 6)[i % 4]][:, 0:HALF]
                if n < 4:
                    A(gT[:, n, f * HALF:(f + 1) * HALF], b, ACT.Sigmoid).then_inc(s_gsig, 1)
                else:
                    A(uT[:, n - 4, PAD + f * HALF:PAD + (f + 1) * HALF], b, ACT.Copy).then_inc(s_uv, 1)

            def v_copy(t):
                R = ROWS[t]
                act.wait_ge(s_qkvm, t + 1)
                if t >= 2:
                    act.wait_ge(s_o, t - 1)
                if t == 4:
                    ch.do(A(v_sb[0:NS, 0, 0:256], bank[0][64:64 + NS, 0:256], ACT.Copy))
                    A(v_sb[0:NS, 0, 256:512], bank[0][96:96 + NS, 0:256], ACT.Copy).then_inc(s_vs, 1)
                    return
                A(v_sb[0:R, t % 2, :], bank[2 * (t % 2) + 1][0:R, :], ACT.Copy).then_inc(s_vs, 1)

            def qkT_copies(t):
                R = ROWS[t]
                act.wait_ge(s_qkT, t + 1)
                if t >= 1:
                    act.wait_ge(s_scm, min(t, 4))
                    act.wait_ge(s_qTd, min(t, 4))
                b = bv(4, 4, R)
                qz = qTz.rearrange("p (a b) i -> p a b i", b=2)
                ch.do(A(qz[0:64, :, 0, 0:R], b[0:64, 0:2, :], ACT.Copy))
                A(qz[64:128, :, 1, 0:R], b[64:128, 0:2, :], ACT.Copy).then_inc(s_qTz, 1)
                A(kT[:, :, 0:R], b[:, 2:4, :], ACT.Copy).then_inc(s_kTs, 1)

            act.wait_ge(s_u8m, 1)
            A(u8, bank[4][0:NS, :], ACT.Copy).then_inc(s_u8, 1)
            act.wait_ge(s_ulm, 1)
            A(hb[0:BUF, 1, 0:512], bank[5][0:BUF, :], ACT.Copy).then_inc(s_ul, 1)
            act.wait_ge(s_zero_q, 1)
            v_copy(0)
            act.wait_ge(s_p8m, 1)
            A(pT[:, :, SEQ:NTOK], bv(7, 4, NS), ACT.Copy).then_inc(s_p8s, 1)
            for t in range(4):
                qkT_copies(t)
                if t == 3:
                    v_copy(4)
                act.wait_ge(s_lv, t + 1)
                A(lrs, lrs, ACT.Sqrt).then_inc(s_ls, 1)
                if t < 3:
                    v_copy(t + 1)

            def pool_copy(i):
                g, f = i // 2, i % 2
                if i == 0:
                    act.wait_ge(s_wpool, 32)
                    act.wait_ge(s_pool, 4)
                act.wait_ge(s_pm, i + 1)
                A(catT[:, 4 + g, f * HALF:(f + 1) * HALF], bank[(2, 5)[i % 2]][:, 0:HALF], ACT.Copy,
                  scale=pscale[:, g:g + 1]).then_inc(s_pc, 1)

            pool_copy(0)
            pool_copy(1)
            act.wait_ge(s_p8, 1)
            broadcast_copies(2, bcG)
            broadcast_copies(3, bcA)
            pool_copy(2)
            pool_copy(3)
            qkT_copies(4)
            for i in range(4, 8):
                pool_copy(i)
            act.wait_ge(s_lv, 5)
            A(lrs[0:NS], lrs[0:NS], ACT.Sqrt).then_inc(s_ls, 1)
            act.wait_ge(s_rot, 5)
            act.wait_ge(s_consts, 16)
            A(ones16, const("ones"), ACT.Copy)
            A(tri16, const("tri"), ACT.Copy).then_inc(s_ones, 1)
            broadcast_copies(4, bcB)
            for t in range(NT):
                R = ROWS[t]
                act.wait_ge(s_x2, 2 * t + 2)
                A(squares[0:R, :], x_sb[0:R, t, :], ACT.Square, accum_out=ss[0:R, t:t + 1]).then_inc(s_ssq2, 1)
                act.wait_ge(s_var2, t + 1)
                A(rstd[0:R, t:t + 1], rstd[0:R, t:t + 1], ACT.Sqrt).then_inc(s_std2, 1)
                if t >= 1:
                    hT_copies(ROWS[t - 1], t - 1, s_h2Ts, s_h2T)
            hT_copies(NS, 4, s_h2Ts, s_h2T)
            act.wait_ge(s_rm, 1)
            act.wait_ge(s_rzero, 1)
            for t in range(NT):
                R = ROWS[t]
                A(scores[0:R, t, :], bank[6][0:R, t * NE:(t + 1) * NE], ACT.Sigmoid).then_inc(s_scr, 1)

            def gate_sigmoid(n, R, par):
                act.wait_ge(s_gm, n + 1)
                if not (isinstance(n, int) and n < 2):
                    act.wait_ge(s_a, n - 1)
                if R == NS:
                    ch.do(A(act_sg[0:NS, par, 0:P], bank[par][0:NS, 0:P], ACT.Sigmoid))
                    A(act_sg[0:NS, par, P:EF], bank[par][32:32 + NS, 0:P], ACT.Sigmoid).then_inc(s_sg, 1)
                    return
                A(act_sg[0:R, par, :], bank[par][0:R, 0:EF], ACT.Sigmoid).then_inc(s_sg, 1)

            def aT_copy(n, R, par):
                act.wait_ge(s_aT, n + 1)
                if not (isinstance(n, int) and n < 2):
                    act.wait_ge(s_dm, n - 1)
                A(aT[:, par, :, 0:R], bank[6][:, 0:256].rearrange("p (k r) -> p k r", k=2)[:, :, 0:R],
                  ACT.Copy).then_inc(s_aTs, 1)

            def y_copy(n, R, par, before=None):
                act.wait_ge(s_dm, n + 1)
                wait_y_free(act, n, before)
                if R == NS:
                    ch.do(A(Y[0:NS, par, 0:256], bank[2][0:NS, 0:256], ACT.Copy))
                    A(Y[0:NS, par, 256:512], bank[2][32:32 + NS, 0:256], ACT.Copy).then_inc(s_ya, 1)
                    return
                A(Y[0:R, par, 0:512], bank[2][0:R, :], ACT.Copy).then_inc(s_ya, 1)

            def xT_copy(w, par):
                act.wait_ge(s_xT, w + 1)
                if not (isinstance(w, int) and w < 2):
                    act.wait_ge(s_gm, w + NT - 1)
                for i in range(2):
                    ins = A(xgT[par][:, 4 * i:4 * i + 4, :], bv(4 + i, 4, P), ACT.Copy)
                    if i == 1:
                        ins.then_inc(s_xTs, 1)

            gate_sigmoid(0, P, 0)
            gate_sigmoid(1, P, 1)
            aT_copy(0, P, 0)
            y_copy(0, P, 0)
            gate_sigmoid(2, P, 0)
            aT_copy(1, P, 1)
            y_copy(1, P, 1)
            gate_sigmoid(3, P, 1)
            aT_copy(2, P, 0)
            y_copy(2, P, 0)
            gate_sigmoid(4, NS, 0)
            aT_copy(3, P, 1)
            y_copy(3, P, 1)
            broadcast_copies(5, bcG)
            xT_copy(0, 0)

            def item(w, par, first=False):
                n = w + NT
                np_ = (par + NT) % 2
                R = NS if first else P
                aT_copy(n - 1, R, 1 - np_)
                gate_sigmoid(n, P, np_)
                xT_copy(w + 1, 1 - par)
                y_copy(n - 1, R, 1 - np_, None if isinstance(w, int) and w < 3 else w - 2)

            item(0, 0, first=True)
            for w in range(1, 4):
                item(w, w % 2)
            act.wait_ge(s_table, 1)
            more = act.value_load(nquad[0:1, 0:1], min_val=NE // 4 - 1, max_val=(NE + MAX_OVER - 1) // 4)
            with act.Fori(1, more + 1) as i:
                for q in range(4):
                    item(i * 4 + q, q % 2)
            aT_copy(more * 4 + (NT + 3), P, 0)
            y_copy(more * 4 + (NT + 3), P, 0, more * 4 + 2)

            def out_rows(t):
                R = ROWS[t]
                act.wait_ge(s_frs, t + 1)
                act.wait_ge(s_xn, t + 1)
                A(yin[0:R, t, :], yin[0:R, t, :], ACT.Copy, scale=rstd[0:R, t:t + 1]).then_inc(s_out, 1)

            for t in range(NT):
                R = ROWS[t]
                act.wait_ge(s_x3, t + 1)
                A(squares_end[0:R, :], x_sb[0:R, t, :], ACT.Square, accum_out=ss[0:R, t:t + 1]).then_inc(s_fs, 1)
                act.wait_ge(s_fv, t + 1)
                A(rstd[0:R, t:t + 1], rstd[0:R, t:t + 1], ACT.Sqrt).then_inc(s_fsd, 1)
                if t >= 1:
                    out_rows(t - 1)
            out_rows(NT - 1)

        @blk.vector
        def _(dve):
            V = nc.vector
            TT, TS, STT = V.tensor_tensor, V.tensor_scalar, V.scalar_tensor_tensor
            ch = Chain(dve, s_dp)
            V.memset(ss, 1.0).then_inc(s_init, 1)
            dve.wait_ge(s_sig_c, 1)
            TT(c_sb, c_sb, c_sg, ALU.mult).then_inc(s_cs, 1)
            dve.wait_ge(s_nrm, 32)
            dve.wait_ge(s_bada, 16)

            def add_ada(c):
                dve.wait_ge(s_adam, c + 1)
                n = ADA_ORDER[c]
                m = mod[0:9, n * 512:(n + 1) * 512]
                for j in range(3):
                    ch.link(TT(m, m, bank[ADA_BANK[c]][32 * j:32 * j + 9, :], ALU.add))
                ins = TT(m, m, bank[ADA_BANK[c]][96:105, :], ALU.add)
                if n // 2 in (1, 4):
                    ch.link(ins)
                    norm = nrm[:, 0 if n // 2 == 1 else 1, (n % 2) * 512:(n % 2 + 1) * 512]
                    ins = STT(out=m, in0=m, scalar=1.0, in1=norm, op0=ALU.add, op1=ALU.mult)
                ins.then_inc(s_modv, 1)

            def variance(cols, squares_done, n, var_done, std_done, m):
                dve.wait_ge(squares_done, n)
                TS(rstd[:, cols], ss[:, cols], 1.0 / D, EPS, ALU.mult, ALU.add).then_inc(var_done, 1)
                dve.wait_ge(std_done, m)

            for c in range(4):
                add_ada(c)
            variance(slice(0, NT), s_ssq, NT, s_var, s_std, 1)
            ch.link(V.reciprocal(rstd[:, 0:NT], rstd[:, 0:NT]))

            def h_rows(t, scale, shift, done, shift_broadcast=None):
                R = ROWS[t]
                ch.link(STT(out=hb[0:R, t % 2, :], in0=x_sb[0:R, t, :], scalar=rstd[0:R, t:t + 1], in1=scale,
                            op0=ALU.mult, op1=ALU.mult))
                if shift_broadcast is not None:
                    dve.wait_ge(s_bcs, shift_broadcast)
                TT(hb[0:R, t % 2, :], hb[0:R, t % 2, :], shift, ALU.add).then_inc(done, 1)

            dve.wait_ge(s_bcs, 2)
            dve.wait_ge(s_modv, 4)
            for t in range(NT):
                if t >= 2:
                    dve.wait_ge(s_hTm, t - 1)
                h_rows(t, bcA if t < 4 else seg(1, NS), bcB if t < 4 else seg(0, NS), s_hb, 4)
            for i in range(8):
                n, f = i // 2, i % 2
                dve.wait_ge(s_gsig, i + 1)
                g = gT[:, n, f * HALF:(f + 1) * HALF]
                TT(g, g, bank[(0, 1, 2, 6)[i % 4]][:, 0:HALF], ALU.mult).then_inc(s_gv, 1)
                if i in (1, 5):
                    add_ada(4 + i // 4)
            add_ada(6)
            dve.wait_ge(s_rows, 64)
            for g in range(4):
                ch.do(V.tensor_reduce(psum8[:, g * P:(g + 1) * P], pool_rows[g].rearrange("p (r c) -> p c r", c=P), AX_X, ALU.add))
            add_ada(7)
            dve.wait_ge(s_gum, 16)
            ch.do(V.memset(qTz, 0.0))
            V.memset(St, 0.0).then_inc(s_zero_q, 1)
            dve.wait_ge(s_zero_q, 1)

            def rotate(t):
                R = ROWS[t]
                dve.wait_ge(s_qkvm, t + 1)
                src = bank[2 * (t % 2)][0:R, :].rearrange("p (c h d) -> p c h d", c=2, h=H)
                t1 = rt[0:R, 0, :].rearrange("p (c h d) -> p c h d", c=2, h=H)
                t2 = rt[0:R, 1, :].rearrange("p (c h d) -> p c h d", c=2, h=H)

                def turn(c, a, b):
                    return rope[0:R, t, c, :, a:b].unsqueeze(2).broadcast_to([R, 2, H, b - a])

                if t == 4:
                    for c in range(2):
                        src = bank[0][32 * c:32 * c + NS, 0:256].rearrange("p (h d) -> p h d", h=H)

                        def turn1(i, a, b):
                            return rope[0:NS, 4, i, c, a:b].unsqueeze(1).broadcast_to([NS, H, b - a])

                        ch.do(TT(t1[:, c], src, turn1(0, 0, QK), ALU.mult))
                        ch.do(TT(t2[:, c, :, 0:32], src[:, :, 32:64], turn1(1, 0, 32), ALU.mult))
                        ch.do(TT(t2[:, c, :, 32:64], src[:, :, 0:32], turn1(1, 32, 64), ALU.mult))
                else:
                    ch.do(TT(t1, src, turn(0, 0, QK), ALU.mult))
                    ch.do(TT(t2[:, :, :, 0:32], src[:, :, :, 32:64], turn(1, 0, 32), ALU.mult))
                    ch.do(TT(t2[:, :, :, 32:64], src[:, :, :, 0:32], turn(1, 32, 64), ALU.mult))
                ch.settle()
                TT(qk_sb[0:R, t % 2, :], rt[0:R, 0, :], rt[0:R, 1, :], ALU.add).then_inc(s_rot, 1)
                if t < 4:
                    dve.wait_ge(s_rot, t + 1)
                    TT(kd.rearrange("p (h d) -> p h d", h=H), qk_sb[:, t % 2, 256:512].rearrange("p (h d) -> p h d", h=H),
                       const("kdec").unsqueeze(2).broadcast_to([P, H, QK]), ALU.mult).then_inc(s_kd, 1)

            def o_norm_start(t):
                R = ROWS[t]
                for h in range(H):
                    ch.do(V.bn_stats(bst[0:R, h, :], bank[6][0:R, h * P:(h + 1) * P]))
                ch.settle()
                for h in range(H):
                    ch.do(V.bn_aggr(mv[0:R, h, :], bst[0:R, h, :]))
                ch.settle()
                TS(lrs[0:R, :], mv[0:R, :, 1], EPS, None, ALU.add).then_inc(s_lv, 1)

            def o_norm_end(t):
                R = ROWS[t]
                dve.wait_ge(s_ls, t + 1)
                ch.link(V.reciprocal(lrs[0:R, :], lrs[0:R, :]))
                if t >= 1:
                    dve.wait_ge(s_oT, t)
                for h in range(H):
                    ins = TS(on[0:R, h * P:(h + 1) * P], bank[6][0:R, h * P:(h + 1) * P], mv[0:R, h, 0:1], lrs[0:R, h:h + 1],
                             ALU.subtract, ALU.mult)
                    ch.do(ins) if h < 3 else ins.then_inc(s_on, 1)

            def gate_o(t):
                R = ROWS[t]
                dve.wait_ge(s_oT, t + 1)
                TT(catT[:, 0:4, tcols(t)], bv(4, 4, R), gT[:, :, tcols(t)], ALU.mult).then_inc(s_cat, 1)

            dve.wait_ge(s_u8, 1)
            ch.settle()
            ch.link(TT(psum8, psum8, u8, ALU.add))
            for g, w in enumerate(POOL_W):
                c = slice(g * P, (g + 1) * P)
                ins = STT(out=psum8[:, c], in0=psum8[:, c], scalar=1.0 / w, in1=u8[:, c], op0=ALU.mult, op1=ALU.subtract)
                ch.do(ins) if g < 3 else ins.then_inc(s_p8, 1)
            dve.wait_ge(s_gv, 8)
            dve.wait_ge(s_consts, 16)
            rotate(0)
            for t in range(4):
                dve.wait_ge(s_qTz, t + 1)
                if t >= 1:
                    dve.wait_ge(s_o, t)
                TT(qTd.rearrange("p (a b) i -> p a b i", b=2), qTz.rearrange("p (a b) i -> p a b i", b=2),
                   qdec.unsqueeze(2).broadcast_to([P, 2, 2, P]), ALU.mult).then_inc(s_qTd, 1)
                dve.wait_ge(s_scm, t + 1)
                TT(scT, bv(5, 4, P), dmat, ALU.mult).then_inc(s_sc, 1)
                if t == 3:
                    rotate(4)
                    dve.wait_ge(s_rot, 5)
                    dve.wait_ge(s_pool, 4)
                    TT(kd8, qk_sb[0:NS, 0, 256:512].unsqueeze(1).broadcast_to([NS, NS, 256]),
                       ident[0:NS, 0:NS].unsqueeze(2).broadcast_to([NS, NS, 256]), ALU.mult).then_inc(s_k8, 1)
                dve.wait_ge(s_o, t + 1)
                o_norm_start(t)
                if t >= 1:
                    dve.wait_ge(s_stv, 4 * t)
                for a in range(2):
                    for b in range(2):
                        r = slice(64 * b, 64 * b + 64)
                        STT(out=St[r, a, :], in0=St[r, a, :], scalar=gam[r, 0, a:a + 1],
                            in1=bank[7][r, a * 256 + b * P:a * 256 + (b + 1) * P], op0=ALU.mult, op1=ALU.add).then_inc(s_stv, 1)
                o_norm_end(t)
                if t < 3:
                    rotate(t + 1)
                gate_o(t)
            dve.wait_ge(s_state, 64)
            for i in range(8):
                a, s2 = i // 4, i % 4
                dve.wait_ge(s_outer, i + 1)
                bo = bv(i % 2, 2, 256)
                for b in range(2):
                    r = slice(64 * b, 64 * b + 64)
                    s_new = S0[r, 2 * s2:2 * s2 + 2, a, :]
                    STT(out=s_new, in0=s_new, scalar=gam[r, 1, a:a + 1], in1=bo[r, :, b * P:(b + 1) * P],
                        op0=ALU.mult, op1=ALU.add).then_inc(s_snew, 1)
                if i == 3:
                    add_ada(8)
                if i == 5:
                    dve.wait_ge(s_qTz, 5)
                    TT(qTm.rearrange("p h (s m) -> p h s m", m=8), qTz[:, :, 0:NS].unsqueeze(2).broadcast_to([P, H, 8, 8]),
                       const("eye8").rearrange("p (s m) -> p s m", m=8).unsqueeze(1).broadcast_to([P, H, 8, 8]), ALU.mult).then_inc(s_qm, 1)
            add_ada(9)
            dve.wait_ge(s_o, 5)
            o_norm_start(4)
            o_norm_end(4)
            gate_o(4)
            V.memset(scores, 0.0).then_inc(s_rzero, 1)

            dve.wait_ge(s_bcs, 10)
            dve.wait_ge(s_modv, 10)
            dve.wait_ge(s_cat, NT)
            dve.wait_ge(s_store, 16 * 8)
            for t in range(NT):
                R = ROWS[t]
                dve.wait_ge(s_wo, t + 1)
                g1 = bcG if t < 4 else seg(2, NS)
                for j in range(4 if t == 4 else 0):
                    c = slice(j * 256, (j + 1) * 256)
                    ch.do(TT(wo_g[0:NS, j // 2, j % 2 * 256:j % 2 * 256 + 256], bank[2][32 * j:32 * j + NS, 0:256], g1[:, c], ALU.mult))
                for f in range(2 if t < 4 else 0):
                    c = slice(f * 512, (f + 1) * 512)
                    ch.do(TT(wo_g[0:R, f, :], bank[2 * ((t + 1) % 2) + f][0:R, :], g1[:, c], ALU.mult))
                ch.settle()
                for f in range(2):
                    c = slice(f * 512, (f + 1) * 512)
                    TT(x_sb[0:R, t, c], x_sb[0:R, t, c], wo_g[0:R, f, :], ALU.add).then_inc(s_x2, 1)
                variance(slice(t, t + 1), s_ssq2, t + 1, s_var2, s_std2, t + 1)
                ch.link(V.reciprocal(rstd[:, t:t + 1], rstd[:, t:t + 1]))
                if t >= 2:
                    dve.wait_ge(s_h2T, t - 1)
                    dve.wait_ge(s_h2st[t % 2], 16 * (t // 2))
                h_rows(t, bcA if t < 4 else seg(4, NS), bcB if t < 4 else seg(3, NS), s_h2)

            dve.wait_ge(s_scr, NT)
            dve.wait_ge(s_sca, 16)
            ch.link(TT(biased, scores, rbias.unsqueeze(1).broadcast_to([P, NT, NE]), ALU.add))
            g8 = biased.rearrange("p t (g m) -> p (t g) m", m=8)
            ch.do(TT(top_a, g8[:, :, 0:4], g8[:, :, 4:8], ALU.max))
            ch.link(TT(top_b, g8[:, :, 0:4], g8[:, :, 4:8], ALU.min))
            ch.do(TT(top_c, top_a[:, :, 0:2], top_a[:, :, 2:4], ALU.max))
            ch.do(TT(top_d, top_a[:, :, 0:2], top_a[:, :, 2:4], ALU.min))
            ch.link(TT(top_e, top_b[:, :, 0:2], top_b[:, :, 2:4], ALU.max))
            ch.link(TT(top_d, top_d, top_e, ALU.max))
            ch.do(TT(top_f[:, :, 0:1], top_c[:, :, 0:1], top_c[:, :, 1:2], ALU.min))
            ch.do(TT(top_f[:, :, 1:2], top_d[:, :, 0:1], top_d[:, :, 1:2], ALU.max))
            ch.do(TT(top_e[:, :, 0:1], top_c[:, :, 0:1], top_c[:, :, 1:2], ALU.max))
            ch.settle()
            ch.link(TT(top_e[:, :, 1:2], top_f[:, :, 0:1], top_f[:, :, 1:2], ALU.max))
            gflat = gs.rearrange("p t g -> p (t g)").unsqueeze(2)
            ch.link(TT(gflat, top_e[:, :, 0:1], top_e[:, :, 1:2], ALU.add))
            mine = gs.unsqueeze(3).broadcast_to([P, NT, 8, 8])
            other = gs.unsqueeze(2).broadcast_to([P, NT, 8, 8])
            ch.do(TT(cmp, other, mine, ALU.is_gt))
            ch.link(TT(cmp2, other, mine, ALU.is_equal))
            ch.link(TT(cmp2, cmp2, const("before").rearrange("p (a b) -> p a b", b=8).unsqueeze(1).broadcast_to([P, NT, 8, 8]), ALU.mult))
            ch.link(TT(cmp, cmp, cmp2, ALU.add))
            ch.link(V.tensor_reduce(rank, cmp, AX_X, ALU.add))
            ch.link(TS(rank, rank, 3.5, NEG, ALU.is_gt, ALU.mult))
            ch.link(TT(g8, g8, rank.rearrange("p t g -> p (t g)").unsqueeze(2).broadcast_to([P, 40, 8]), ALU.add))
            for t in range(NT):
                ch.do(V.max(v8[:, t, :], biased[:, t, :]))
            ch.settle()
            for t in range(NT):
                ch.do(V.match_replace(rep[:, t, :], v8[:, t, :], biased[:, t, :], 3.0 * NEG))
            ch.settle()
            ch.link(TT(rep, rep, biased, ALU.not_equal))
            TT(msk, rep, const("rowok").unsqueeze(2).broadcast_to([P, NT, NE]), ALU.mult).then_inc(s_msk, 1)

            def gated(n, R, par, gate=None):
                dve.wait_ge(s_sg, n + 1)
                if not (isinstance(n, int) and n < 2):
                    dve.wait_ge(s_aT, n - 1)
                c = loop[0]
                if R == NS:
                    for j in range(2):
                        cols = slice(j * P, (j + 1) * P)
                        c.link(TT(act_t[0:NS, par, cols], act_sg[0:NS, par, cols], bank[par][32 * j:32 * j + NS, 0:P], ALU.mult))
                        ins = TT(act_a[0:NS, par, cols], act_t[0:NS, par, cols], bank[par][64 + 32 * j:64 + 32 * j + NS, 0:P], ALU.mult)
                        c.do(ins) if j == 0 else ins.then_inc(s_a, 1)
                    return
                c.link(TT(act_t[0:R, par, :], act_sg[0:R, par, :], bank[par][0:R, 0:EF], ALU.mult))
                if gate is None:
                    ins = TT(act_a[0:R, par, :], act_t[0:R, par, :], bank[par][0:R, EF:2 * EF], ALU.mult)
                else:
                    ins = STT(out=act_a[0:R, par, :], in0=act_t[0:R, par, :], scalar=gate, in1=bank[par][0:R, EF:2 * EF],
                              op0=ALU.mult, op1=ALU.mult)
                ins.then_inc(s_a, 1)

            def y_copy(n, R, par, before=None):
                dve.wait_ge(s_dm, n + 1)
                wait_y_free(dve, n, before)
                if R == NS:
                    loop[0].do(V.tensor_copy(Y[0:NS, par, 512:768], bank[2][64:64 + NS, 0:256]))
                    V.tensor_copy(Y[0:NS, par, 768:1024], bank[2][96:96 + NS, 0:256]).then_inc(s_yb, 1)
                    return
                V.tensor_copy(Y[0:R, par, 512:1024], bank[3][0:R, :]).then_inc(s_yb, 1)

            loop = [ch]
            gated(0, P, 0)
            dve.wait_ge(s_msk, 1)
            dve.wait_ge(s_posm, 1)
            pos_bank = bank[7][:, 0:NT * NE].rearrange("p (t e) -> p t e", e=NE)
            ch.link(STT(out=posm.rearrange("p t e -> p (t e)"), in0=bank[7][:, 0:NT * NE], scalar=1.0,
                        in1=msk.rearrange("p t e -> p (t e)"), op0=ALU.add, op1=ALU.mult))
            ch.link(TS(posm, posm, 1.0, None, ALU.subtract))
            ch.link(V.tensor_copy(cnt[:, 0:1], bank[7][0:NE, 320:321]))
            ch.link(TT(present, cnt[:, 0:1].broadcast_to([NE, 4]), const("bmul", rows=NE), ALU.is_gt))
            V.tensor_reduce(cnt[:, 1:2], present, AX_X, ALU.add).then_inc(s_ovx, 1)
            gated(1, P, 1)
            add_ada(10)
            y_copy(0, P, 0)
            dve.wait_ge(s_ovm, 1)
            ch.link(V.tensor_copy(cnt[:, 2:3], bank[7][0:NE, 384:385]))
            ch.link(TS(place_o, const("bm", rows=NE), cnt[:, 2:3], None, ALU.add))
            ch.link(TT(over, const("islot", rows=NE).unsqueeze(1).broadcast_to([NE, 4, 40]),
                       place_o.unsqueeze(2).broadcast_to([NE, 4, 40]), ALU.is_equal))
            ch.link(TT(over, over, present.unsqueeze(2).broadcast_to([NE, 4, 40]), ALU.mult))
            ch.link(V.tensor_reduce(ov_w[:, 0, :], over.rearrange("p b s -> p s b"), AX_X, ALU.add))
            ch.link(TS(place_o, const("bmul", rows=NE), float(NO_SLOT), None, ALU.subtract))
            ch.link(TT(over, over, place_o.unsqueeze(2).broadcast_to([NE, 4, 40]), ALU.mult))
            V.tensor_reduce(ov_w[:, 1, :], over.rearrange("p b s -> p s b"), AX_X, ALU.add).then_inc(s_ovw, 1)
            add_ada(11)
            gated(2, P, 0)
            y_copy(1, P, 1)
            ch.link(TT(gates, scores, msk, ALU.mult))
            ch.link(V.tensor_reduce(gsum[:, 0:NT], gates, AX_X, ALU.add))
            ch.link(TS(gsum[:, 0:NT], gsum[:, 0:NT], 1e-30, None, ALU.max))
            ch.link(V.reciprocal(gsum[:, 0:NT], gsum[:, 0:NT]))
            ch.link(TT(gates, gates, gsum[:, 0:NT].unsqueeze(2).broadcast_to([P, NT, NE]), ALU.mult))
            ch.link(TS(gates, gates, 2.5, None, ALU.mult))
            ch.link(V.tensor_copy(gate_parts[:, :, 0, :], gates))
            ch.link(TT(gate_rest, gates, gate_parts[:, :, 0, :], ALU.subtract))
            ch.link(V.tensor_copy(gate_parts[:, :, 1, :], gate_rest))
            ch.link(TT(gate_parts[:, :, 2, :], gate_rest, gate_parts[:, :, 1, :], ALU.subtract))
            ch.do(V.tensor_copy(tablef[:, 0, 0:NE], const("iota", NE, rows=1)))
            ch.do(V.memset(tablef[:, 1, 0:NE], 0.0))
            dve.wait_ge(s_tm, 1)
            ch.do(V.tensor_copy(tablef[:, 0, NE:NITEM], bank[7][0:1, 388:428]))
            ch.do(TS(tablef[:, 1, NE:NITEM], bank[7][0:1, 428:468], float(NO_SLOT), None, ALU.add))
            ch.do(TS(nquad[:, 1:2], bank[7][0:1, 468:469], 3.0, None, ALU.add))
            ch.settle()
            ch.do(V.tensor_copy(table, tablef))
            ch.do(TS(nquad[:, 2:3], nquad[:, 1:2], 2, None, ALU.logical_shift_right))
            for i in range(2):
                ch.do(V.tensor_copy(info[i][:, :, 0:3], tokc))
            ch.settle()
            TS(nquad[:, 0:1], nquad[:, 2:3], float(NE // 4 - 1), None, ALU.add).then_inc(s_table, 1)
            dve.wait_ge(s_table, 1)

            def choose(w, par, e, base):
                if not (isinstance(w, int) and w < 2):
                    dve.wait_ge(s_selm, w - 1)
                c = loop[0]
                c.do(TT(sel[par], iota[:, ds(base, P)].unsqueeze(1).broadcast_to([P, NT, P]),
                        posm[:, :, ds(e, 1)].broadcast_to([P, NT, P]), ALU.is_equal))
                V.tensor_copy(info[par][:, :, 3:6].unsqueeze(3), gate_parts[:, :, :, ds(e, 1)]).then_inc(s_sel, 1)

            def rows_of(w, par):
                dve.wait_ge(s_selm, w + 1)
                if not (isinstance(w, int) and w < 2):
                    dve.wait_ge(s_gat[par], (w - par) * 8)
                c = loop[0]
                c.link(V.tensor_reduce(got[:, par, :], bank[7][:, 0:6].rearrange("p (a b) -> p a b", b=3), AX_X, ALU.add))
                TS(gidx[:, par:par + 1], got[:, par, 0:1], float(FAR), None, ALU.add).then_inc(s_idx, 1)

            def take_rows(w, par):
                dve.wait_ge(s_idx, w + 1)
                if not (isinstance(w, int) and w < 2):
                    dve.wait_ge(s_sidx, w - 1)
                    dve.wait_ge(s_a, w + NT - 1)
                c = loop[0]
                c.do(V.tensor_copy(midx[:, par:par + 1], gidx[:, par:par + 1]))
                c.link(V.tensor_copy(mgate[:, par:par + 1], got[:, par, 1:2]))

            def keep_rows(w, par):
                if not (isinstance(w, int) and w < 2):
                    dve.wait_ge(s_sca, (w - 1) * 16 + 16)
                V.tensor_copy(sidx[:, par:par + 1], midx[:, par:par + 1]).then_inc(s_sidx, 1)

            choose(0, 0, 0, 0)
            gated(3, P, 1)
            choose(1, 1, 1, 0)
            y_copy(2, P, 0)
            rows_of(0, 0)
            choose(2, 0, 2, 0)
            gated(4, NS, 0)
            y_copy(3, P, 1)
            rows_of(1, 1)

            def item(w, par, first=False):
                n = w + NT
                np_ = (par + NT) % 2
                take_rows(w, par)
                rows_of(w + 2, par)
                gated(n, P, np_, mgate[:, par:par + 1])
                y_copy(n - 1, NS if first else P, 1 - np_, None if isinstance(w, int) and w < 3 else w - 2)
                keep_rows(w, par)
                if isinstance(w, int):
                    choose(w + 3, 1 - par, w + 3, 0)
                else:
                    e = dve.value_load(table[0:1, 0, ds(w + 3, 1)], min_val=0, max_val=NE - 1)
                    base = dve.value_load(table[0:1, 1, ds(w + 3, 1)], min_val=0, max_val=NO_SLOT)
                    choose(w + 3, 1 - par, e, base)

            item(0, 0, first=True)
            for w in range(1, 4):
                item(w, w % 2)
            more = dve.value_load(nquad[0:1, 0:1], min_val=NE // 4 - 1, max_val=(NE + MAX_OVER - 1) // 4)
            STEPS = 20
            with dve.Fori(1, more + 1) as i:
                loop[0] = Chain(dve, s_dl, i * STEPS - STEPS)
                for q in range(4):
                    item(i * 4 + q, q % 2)
                assert loop[0].n == STEPS, loop[0].n
            y_copy(more * 4 + (NT + 3), P, 0, more * 4 + 2)

            ch = Chain(dve, s_de)
            dve.wait_ge(s_bcs, 12)

            def x3_rows(t):
                R = ROWS[t]
                dve.wait_ge(s_yin[t], 16)
                y = yin[0:R, t, :]
                ch.link(TT(y, y, bcG if t < 4 else seg(5, NS), ALU.mult))
                TT(x_sb[0:R, t, :], x_sb[0:R, t, :], y, ALU.add).then_inc(s_x3, 1)

            x3_rows(0)
            for t in range(NT):
                if t + 1 < NT:
                    x3_rows(t + 1)
                variance(slice(t, t + 1), s_fs, t + 1, s_fv, s_fsd, t + 1)
                V.reciprocal(rstd[:, t:t + 1], rstd[:, t:t + 1]).then_inc(s_frs, 1)


_INS = ["x_prompt", "x_sample", "c_prompt", "c_sample", "state_ret", "state_pool", "norm1", "norm2", "norm_f",
        "w_ada", "b_ada", "w_in", "w_out", "w_pool", "pool_scale", "w_router", "router_bias",
        "w_exp_gate", "w_exp_up", "w_exp_down", "w_sh_gate", "w_sh_up", "w_sh_down"]
_OUTS = {"y_p": (1, SEQ, D), "y_s": (NS, 1, D), "ret_p": (1, 1, H, QK, VD), "pool_p": (1, 1, BUF, 512),
         "ret_s": (1, NS, H, QK, VD), "pool_s": (1, NS, BUF, 512)}


def kernel(**inputs):
    import concourse.bacc as bacc
    from concourse.bass_utils import run_bass_kernel_spmd

    nc = bacc.Bacc("TRN2", target_bir_lowering=False, num_devices=1)
    arrays, I, O = {}, {}, {}
    for name in _INS:
        arrays[f"in_{name}"] = np.ascontiguousarray(inputs[name])
    arrays["in_consts"] = constants()
    for name in _INS + ["consts"]:
        a = arrays[f"in_{name}"]
        I[name] = nc.dram_tensor(f"in_{name}", a.shape, mybir.dt.from_np(a.dtype), kind="ExternalInput").ap()
    for name, shape in _OUTS.items():
        O[name] = nc.dram_tensor(f"out_{name}", shape, F32, kind="ExternalOutput").ap()
    build(nc, I, O)
    r = run_bass_kernel_spmd(nc, [arrays], core_ids=[0])
    return tuple(r.results[0][f"out_{name}"] for name in _OUTS)
```
